# Optimizing a Trainium2 kernel written in Bass

```python
import jax, jax.numpy as jnp
from jax import lax
import numpy as np

D_MODEL = 1024
BATCH = 1
SEQ = 512
DEPTH = 1
DEC_BATCH = 8
DEC_SEQ = 1
PAST_LEN = 1024
PAGE_SIZE = 128

HEAD_DIM = 64
HEADS_PER_GROUP = 4
ATTN_GROUPS = ((128, 1), (512, 4), (2048, 16))
N_GROUPS = 3
N_ATTN_HEADS = HEADS_PER_GROUP * N_GROUPS
ATTN_WIDTH = N_ATTN_HEADS * HEAD_DIM
ATTN_OUT_WIDTH = HEADS_PER_GROUP * HEAD_DIM
BAND_BLOCK = 128
CONV_WIDTH = D_MODEL // 2
CONV_K = 3
N_EXPERT_GROUPS = 4
EXPERTS_PER_GROUP = 8
N_EXPERTS = N_EXPERT_GROUPS * EXPERTS_PER_GROUP
TOP_K_IN_GROUP = 2
EXPERT_FF = D_MODEL // 4
IN_COLS = 3 * ATTN_WIDTH + 3 * CONV_WIDTH + 2 * D_MODEL
RMS_EPS = 1e-6

kernel_name = 'hybrid_dilated_shortconv_hmoe_step'

def _rmsnorm(x, g):
    x32 = x.astype(jnp.float32)
    y = x32 * lax.rsqrt(jnp.mean(x32 * x32, axis=-1, keepdims=True) + RMS_EPS)
    return (y * g.astype(jnp.float32)).astype(x.dtype)

def _alibi_slopes():
    i = jnp.arange(1, N_ATTN_HEADS + 1, dtype=jnp.float32)
    return (2.0 ** (-8.0 * i / N_ATTN_HEADS)).reshape(N_GROUPS, HEADS_PER_GROUP)

def _dilated_band_attention(q, k, v, slopes, window, dilation):
    b, s, h, dh = q.shape
    n_back = window // dilation
    sub_len = s // dilation
    nblk = -(-sub_len // BAND_BLOCK)
    pad_len = nblk * BAND_BLOCK - sub_len

    def blocks(a):
        a = a.astype(jnp.float32).reshape(b, sub_len, dilation, h, dh)
        a = jnp.pad(a, ((0, 0), (0, pad_len), (0, 0), (0, 0), (0, 0)))
        return a.reshape(b, nblk, BAND_BLOCK, dilation, h, dh)

    def band(a):
        a = jnp.pad(blocks(a), ((0, 0), (1, 0), (0, 0), (0, 0), (0, 0), (0, 0)))
        return jnp.concatenate([a[:, :-1], a[:, 1:]], axis=2)

    qb, kb, vb = blocks(q), band(k), band(v)
    qi = jnp.arange(BAND_BLOCK)
    ki = jnp.arange(2 * BAND_BLOCK) - BAND_BLOCK
    delta = qi[:, None] - ki[None, :]
    key_idx = jnp.arange(nblk)[:, None] * BAND_BLOCK + ki[None, :]
    mask = ((delta >= 0) & (delta <= n_back))[None] & (key_idx >= 0)[:, None, :]
    bias = -slopes[:, None, None] * (delta * dilation).astype(jnp.float32)[None]
    sc = jnp.einsum('bnqrhd,bnkrhd->bnrhqk', qb, kb) * (dh ** -0.5) + bias[None, None, None]
    sc = jnp.where(mask[None, :, None, None], sc, -jnp.inf)
    m = jnp.max(sc, axis=-1, keepdims=True)
    e = jnp.exp(sc - m)
    den = jnp.sum(e, axis=-1, keepdims=True)
    o = jnp.einsum('bnrhqk,bnkrhd->bnqrhd', e / den, vb)
    o = o.reshape(b, nblk * BAND_BLOCK, dilation, h, dh)[:, :sub_len].reshape(b, s, h, dh)
    lse = (m + jnp.log(den))[..., 0].transpose(0, 1, 4, 2, 3)
    lse = lse.reshape(b, nblk * BAND_BLOCK, dilation, h)[:, :sub_len].reshape(b, s, h)
    return o, lse

def _dilated_cached_attention(q, k_new, v_new, kv_buf, slopes, window, dilation):
    buf_len = kv_buf.shape[1]
    t = q.shape[1]
    dh = q.shape[-1]
    offs = dilation * jnp.arange(window // dilation + 1)
    rows = buf_len + jnp.arange(t)[:, None] - offs[None, :]
    valid = rows >= 0
    rows = jnp.maximum(rows, 0)
    k_ext = jnp.concatenate([kv_buf[:, :, 0], k_new], axis=1).astype(jnp.float32)
    v_ext = jnp.concatenate([kv_buf[:, :, 1], v_new], axis=1).astype(jnp.float32)
    kg = k_ext[:, rows]
    vg = v_ext[:, rows]
    sc = (jnp.einsum('bthd,btjhd->bhtj', q.astype(jnp.float32), kg) * (dh ** -0.5)
          - slopes[:, None, None] * offs.astype(jnp.float32)[None, None, :])
    sc = jnp.where(valid[None, None], sc, -jnp.inf)
    m = jnp.max(sc, axis=-1, keepdims=True)
    e = jnp.exp(sc - m)
    den = jnp.sum(e, axis=-1, keepdims=True)
    o = jnp.einsum('bhtj,btjhd->bthd', e / den, vg)
    lse = (m + jnp.log(den))[..., 0].transpose(0, 2, 1)
    return o, lse

def _mix_groups(outs, lses, dtype):
    alpha = jax.nn.softmax(jnp.stack(lses, axis=-1), axis=-1)
    o = jnp.einsum('bthg,bthgd->bthd', alpha, jnp.stack(outs, axis=3))
    return o.reshape(o.shape[0], o.shape[1], ATTN_OUT_WIDTH).astype(dtype)

def _causal_conv(u, prefix, conv_w):
    t = u.shape[1]
    ext = jnp.concatenate([prefix, u], axis=1)
    y = sum(conv_w[j] * ext[:, j:j + t] for j in range(CONV_K))
    return y, ext[:, t:]

def _hier_moe(h, w_rg, b_rg, w_re, b_re, w_gate_e, w_up_e, w_down_e):
    bsz, t, _ = h.shape
    lg = (h @ w_rg).astype(jnp.float32) + b_rg.astype(jnp.float32)
    pg = jax.nn.softmax(lg, axis=-1)
    gidx = jnp.argmax(lg, axis=-1)
    p_top = jnp.take_along_axis(pg, gidx[..., None], axis=-1)
    le = ((h @ w_re).astype(jnp.float32) + b_re.astype(jnp.float32)).reshape(bsz, t, N_EXPERT_GROUPS, EXPERTS_PER_GROUP)
    le_sel = jnp.take_along_axis(le, gidx[..., None, None], axis=2)[..., 0, :]
    top_v, top_i = lax.top_k(le_sel, TOP_K_IN_GROUP)
    w_top = jax.nn.softmax(top_v, axis=-1) * p_top
    inner = jnp.einsum('btk,btke->bte', w_top, jax.nn.one_hot(top_i, EXPERTS_PER_GROUP, dtype=jnp.float32))
    combine = jax.nn.one_hot(gidx, N_EXPERT_GROUPS, dtype=jnp.float32)[..., :, None] * inner[..., None, :]
    combine = combine.reshape(bsz, t, N_EXPERTS).astype(h.dtype)
    a = jnp.einsum('btd,edf->btef', h, w_gate_e)
    b = jnp.einsum('btd,edf->btef', h, w_up_e)
    return jnp.einsum('btef,efd->btd', jax.nn.silu(a) * b * combine[..., None], w_down_e)

def _front(x, c, g_mix, w_ada, b_ada, w_in):
    mod = (jax.nn.silu(c) @ w_ada + b_ada)[:, None, :]
    shift1, scale1, gate1, shift2, scale2, gate2 = jnp.split(mod, 6, axis=-1)
    h = _rmsnorm(x, g_mix) * (1 + scale1) + shift1
    aw, cw = ATTN_WIDTH, CONV_WIDTH
    pts = [aw, 2 * aw, 3 * aw, 3 * aw + cw, 3 * aw + 2 * cw, 3 * aw + 3 * cw, 3 * aw + 3 * cw + D_MODEL]
    q, k, v, b_gate, c_gate, u_in, gate_a, gate_b = jnp.split(h @ w_in, pts, axis=-1)
    bsz, t = x.shape[:2]
    q, k, v = (z.reshape(bsz, t, N_GROUPS, HEADS_PER_GROUP, HEAD_DIM) for z in (q, k, v))
    return (q, k, v), c_gate * u_in, b_gate, gate_a, gate_b, (gate1, shift2, scale2, gate2)

def _back(x, mods, o_attn, o_conv, gate_a, gate_b, w_pa, w_pb, w_o, g_ffn,
          w_rg, b_rg, w_re, b_re, w_gate_e, w_up_e, w_down_e):
    gate1, shift2, scale2, gate2 = mods
    merged = jax.nn.sigmoid(gate_a) * (o_attn @ w_pa) + jax.nn.sigmoid(gate_b) * (o_conv @ w_pb)
    x = x + gate1 * (merged @ w_o)
    h = _rmsnorm(x, g_ffn) * (1 + scale2) + shift2
    return x + gate2 * _hier_moe(h, w_rg, b_rg, w_re, b_re, w_gate_e, w_up_e, w_down_e)

def _prompt_layer(x, c, lw):
    g_mix, w_ada, b_ada, w_in, conv_w, *back = lw
    (q, k, v), u, b_gate, gate_a, gate_b, mods = _front(x, c, g_mix, w_ada, b_ada, w_in)
    slopes = _alibi_slopes()
    s = x.shape[1]
    outs, lses, kv_rows = [], [], []
    for g, (window, dilation) in enumerate(ATTN_GROUPS):
        o, lse = _dilated_band_attention(q[:, :, g], k[:, :, g], v[:, :, g], slopes[g], window, dilation)
        outs.append(o)
        lses.append(lse)
        kv_rows.append(jnp.stack([k[:, :, g], v[:, :, g]], axis=2)[:, s - min(window, s):])
    o_attn = _mix_groups(outs, lses, x.dtype)
    y_conv, conv_state = _causal_conv(u, jnp.zeros_like(u[:, :CONV_K - 1]), conv_w)
    y = _back(x, mods, o_attn, b_gate * y_conv, gate_a, gate_b, *back)
    return y, (*kv_rows, conv_state)

def _sample_layer(x, c, kv_bufs, conv_buf, lw):
    g_mix, w_ada, b_ada, w_in, conv_w, *back = lw
    (q, k, v), u, b_gate, gate_a, gate_b, mods = _front(x, c, g_mix, w_ada, b_ada, w_in)
    slopes = _alibi_slopes()
    outs, lses, kv_rows = [], [], []
    for g, ((window, dilation), kv_buf) in enumerate(zip(ATTN_GROUPS, kv_bufs)):
        o, lse = _dilated_cached_attention(q[:, :, g], k[:, :, g], v[:, :, g], kv_buf, slopes[g], window, dilation)
        outs.append(o)
        lses.append(lse)
        kv_rows.append(jnp.stack([k[:, :, g], v[:, :, g]], axis=2))
    o_attn = _mix_groups(outs, lses, x.dtype)
    y_conv, conv_state = _causal_conv(u, conv_buf, conv_w)
    y = _back(x, mods, o_attn, b_gate * y_conv, gate_a, gate_b, *back)
    return y, (*kv_rows, conv_state)

def setup_inputs(seed: int = 0) -> dict:
    key = jax.random.key(seed)
    ks = jax.random.split(key, 28)

    def nrm(k, shape, scale):
        return scale * jax.random.normal(k, shape, jnp.float32)

    def kv_shape(window):
        return (DEPTH, DEC_BATCH, min(window, PAST_LEN), 2, HEADS_PER_GROUP, HEAD_DIM)

    return {
        'x_prompt': nrm(ks[0], (BATCH, SEQ, D_MODEL), 1.0),
        'x_sample': nrm(ks[1], (DEC_BATCH, DEC_SEQ, D_MODEL), 1.0),
        'cache_kv_w128': nrm(ks[2], kv_shape(ATTN_GROUPS[0][0]), 1.0),
        'cache_kv_w512': nrm(ks[3], kv_shape(ATTN_GROUPS[1][0]), 1.0),
        'cache_kv_w2048': nrm(ks[4], kv_shape(ATTN_GROUPS[2][0]), 1.0),
        'cache_conv': nrm(ks[5], (DEPTH, DEC_BATCH, CONV_K - 1, CONV_WIDTH), 1.0),
        'c_prompt': nrm(ks[6], (BATCH, D_MODEL), 1.0),
        'c_sample': nrm(ks[7], (DEC_BATCH, D_MODEL), 1.0),
        'g_mix': 1.0 + nrm(ks[8], (DEPTH, D_MODEL), 0.02),
        'w_ada': nrm(ks[9], (DEPTH, D_MODEL, 6 * D_MODEL), 0.5 * D_MODEL ** -0.5),
        'b_ada': nrm(ks[10], (DEPTH, 6 * D_MODEL), 0.02),
        'w_in': nrm(ks[11], (DEPTH, D_MODEL, IN_COLS), D_MODEL ** -0.5),
        'conv_w': nrm(ks[12], (DEPTH, CONV_K, CONV_WIDTH), CONV_K ** -0.5),
        'w_pa': nrm(ks[13], (DEPTH, ATTN_OUT_WIDTH, D_MODEL), ATTN_OUT_WIDTH ** -0.5),
        'w_pb': nrm(ks[14], (DEPTH, CONV_WIDTH, D_MODEL), CONV_WIDTH ** -0.5),
        'w_o': nrm(ks[15], (DEPTH, D_MODEL, D_MODEL), D_MODEL ** -0.5),
        'g_ffn': 1.0 + nrm(ks[16], (DEPTH, D_MODEL), 0.02),
        'w_router_group': nrm(ks[17], (DEPTH, D_MODEL, N_EXPERT_GROUPS), D_MODEL ** -0.5),
        'b_router_group': nrm(ks[18], (DEPTH, N_EXPERT_GROUPS), 0.01),
        'w_router_expert': nrm(ks[19], (DEPTH, D_MODEL, N_EXPERTS), D_MODEL ** -0.5),
        'b_router_expert': nrm(ks[20], (DEPTH, N_EXPERTS), 0.01),
        'w_gate_e': nrm(ks[21], (DEPTH, N_EXPERTS, D_MODEL, EXPERT_FF), D_MODEL ** -0.5),
        'w_up_e': nrm(ks[22], (DEPTH, N_EXPERTS, D_MODEL, EXPERT_FF), D_MODEL ** -0.5),
        'w_down_e': nrm(ks[23], (DEPTH, N_EXPERTS, EXPERT_FF, D_MODEL), EXPERT_FF ** -0.5),
        'g_final': 1.0 + nrm(ks[24], (D_MODEL,), 0.02),
    }

def reference(x_prompt, x_sample, cache_kv_w128, cache_kv_w512, cache_kv_w2048, cache_conv,
              c_prompt, c_sample, g_mix, w_ada, b_ada, w_in, conv_w, w_pa, w_pb, w_o, g_ffn,
              w_router_group, b_router_group, w_router_expert, b_router_expert,
              w_gate_e, w_up_e, w_down_e, g_final):
    xp, xs = x_prompt, x_sample
    st_p, st_s = [], []
    for l in range(DEPTH):
        lw = (g_mix[l], w_ada[l], b_ada[l], w_in[l], conv_w[l], w_pa[l], w_pb[l], w_o[l], g_ffn[l],
              w_router_group[l], b_router_group[l], w_router_expert[l], b_router_expert[l],
              w_gate_e[l], w_up_e[l], w_down_e[l])
        xp, sp = _prompt_layer(xp, c_prompt, lw)
        xs, ss = _sample_layer(xs, c_sample, (cache_kv_w128[l], cache_kv_w512[l], cache_kv_w2048[l]),
                               cache_conv[l], lw)
        st_p.append(sp)
        st_s.append(ss)
    y_prompt = _rmsnorm(xp, g_final)
    y_sample = _rmsnorm(xs, g_final)
    p_kv128, p_kv512, p_kv2048, p_conv = (jnp.stack(z) for z in zip(*st_p))
    s_kv128, s_kv512, s_kv2048, s_conv = (jnp.stack(z) for z in zip(*st_s))
    return (y_prompt, y_sample, p_kv128, p_kv512, p_kv2048, p_conv, s_kv128, s_kv512, s_kv2048, s_conv)


_drawn_inputs = setup_inputs


def setup_inputs(seed=0):
    import zlib

    import numpy as np

    out = dict(_drawn_inputs(seed))
    spreads = {}
    factors = {'cache_kv_w128': 4.087,
     'cache_kv_w512': 2.921,
     'g_ffn': 4.638,
     'b_router_group': 8.0,
     'b_router_expert': 8.0,
     'g_final': 2.814}
    for name, (base, spread) in spreads.items():
        noise = np.random.default_rng([zlib.crc32(name.encode()), seed]).standard_normal(out[name].shape)
        drawn = base * np.exp(spread * noise) if base else spread * noise
        out[name] = __import__('jax').numpy.asarray(drawn.astype(out[name].dtype))
    for name, factor in factors.items():
        out[name] = (out[name] * factor).astype(out[name].dtype)
    return out
```

```python
from contextlib import ExitStack

import numpy as np

import concourse.bass as bass
from concourse import mybir

F32 = mybir.dt.float32
I32 = mybir.dt.int32
U32 = mybir.dt.uint32
ALU = mybir.AluOpType
ACT = mybir.ActivationFunctionType
AX = mybir.AxisListType

P = 128
D = 1024
KD = D // P
TP = 512
TS = 8
T = TP + TS
NB = TP // P
HALF = T // 2
G, H, DH = 3, 4, 64
AW = G * H * DH
OW = H * DH
CW = D // 2
CF = CW // P
DIL = (1, 4, 16)
WIN = (128, 512, 2048)
PAST = 1024
SLOPE = (2.0 ** (-8.0 * np.arange(1, G * H + 1) / (G * H))).reshape(G, H)
NG, EG = 4, 8
NE = NG * EG
FF = D // 4
FE = FF // P
EPS = 1e-6
SCALE = DH ** -0.5
BIG = 1e30
SKIP = 1.0e6
R = 64
RBITS = R.bit_length() - 1
OVER = 2 * T // (R + 1)
NTILE = NE + OVER
KEYS = tuple(min(w // d, (PAST if w > PAST else w) // d) for w, d in zip(WIN, DIL))

Q0, K0, V0, B0, C0, U0 = 0, AW // P, 2 * AW // P, 3 * AW // P, (3 * AW + CW) // P, (3 * AW + 2 * CW) // P
GA0 = (3 * AW + 3 * CW) // P
GB0 = GA0 + KD
AT = AW // P
ORDER = ([("v", V0 + f, f) for f in range(AT)] + [("k", K0 + f, f) for f in range(AT)]
         + [("q", Q0 + f, f) for f in range(AT)]
         + [x for f in range(CF) for x in (("c", C0 + f, f), ("u", U0 + f, f))]
         + [("b", B0 + f, f) for f in range(CF)]
         + [x for f in range(KD) for x in (("ga", GA0 + f, f), ("gb", GB0 + f, f))])
NQKV = 3 * AT
NCONV = NQKV + 3 * CF
NEARLY = NCONV + 4
WRING = 4
UNITS = [(b, h) for b in range(NB) for h in range(H)]
ERING = 5
EUN = 4
AHEAD = EUN - 1


def segments(b):
    out = []
    for g in range(G):
        lo = max(0, b - 1) * P if g == 0 else 0
        out.append((lo, (b + 1) * P - lo))
    return out


def hybrid_step(nc, x_prompt, x_sample, kv0, kv1, kv2, cache_conv, c_prompt, c_sample, g_mix, w_ada, b_ada, w_in,
                conv_w, w_pa, w_pb, w_o, g_ffn, w_rg, b_rg, w_re, b_re, w_gate, w_up, w_down, g_final,
                y_prompt, y_sample, p_kv128, p_kv512, p_kv2048, p_conv, s_kv128, s_kv512, s_kv2048, s_conv):
    ctx = ExitStack()
    with ctx:
        ctx.enter_context(nc.allow_non_contiguous_dma(reason="small vectors"))

        def sem(name):
            return ctx.enter_context(nc.semaphore(name))


        layout, at = {}, 0
        for name, n in (("X", 5 * D), ("M", 9 * D), ("RING", WRING * D), ("UC", CF * (T + 2)), ("YC", CF * T),
                        ("CT", 2 * T), ("CACHE", 6 * D), ("HT", KD * T), ("VTOK", 5 * AW), ("VST", 2 * T),
                        ("ADA", 4 * D), ("QK", 2 * AT * T), ("SMALL", 4040)):
            layout[name] = at
            at += n
        arena = ctx.enter_context(nc.sbuf_tensor("arena", [P, at], F32))

        def region(name, off, n, rows=P):
            return arena[0:rows, layout[name] + off:layout[name] + off + n]

        def cube(ap, n):
            return ap.rearrange("p (a b) -> p a b", a=n)

        x = cube(region("X", 0, 5 * D), 5)
        ktok = cube(region("X", 0, 5 * AW), 5)
        prob = cube(region("X", 0, 2 * 1280), 2)
        probT = cube(region("X", 2560, 2 * 512), 2)
        attnT = cube(region("X", 3584, 2 * T), 2)
        otok = region("X", 3584 + 2 * T, OW)
        bias = cube(region("M", 0, 5 * D), H)
        qb = region("M", 5 * D, 2 * D)
        ada_bias = cube(region("M", 5 * D, 12 * P), 12)
        mods = cube(region("M", 7 * D, 12 * P), 12)
        biasS = region("M", 7 * D, H * G * P, TS).rearrange("p (h g r) -> p h g r", h=H, g=G)
        mod_p = cube(region("M", 0, 4 * D), 4)
        mod_s = cube(region("M", 4 * D, 4 * D, TS), 4)
        gffn_b = region("M", 8 * D, D)
        ring = region("RING", 0, WRING * D).rearrange("p (s k n) -> p s k n", s=WRING, k=KD)
        uT = cube(region("UC", 0, CF * (T + 2)), CF)
        yT = cube(region("YC", 0, CF * T), CF)
        cgate = region("CT", 0, T)
        ustate = region("CT", T, CW, 2 + TS)
        modT = cube(region("CT", 0, 4 * P), 4)
        selfp = region("VST", 0, AW, TS)
        selfs = region("VST", AW, OW, TS)
        g8 = region("CT", T, P, KD)
        ccrow = region("YC", 0, CW, 19)
        cache = cube(region("CACHE", 0, 6 * D), G)
        wpa = cube(region("CACHE", 0, 2 * D), 2)
        wpb = cube(region("CACHE", 2 * D, 4 * D), CF)
        hT = cube(region("HT", 0, KD * T), KD)
        vtok = cube(region("VTOK", 0, 5 * AW), 5)
        vst = cube(region("VST", 0, 2 * T), 2)
        crow = region("VST", 0, D, 1 + TS)
        wo = [cube(region("VTOK", 0, 4 * D), KD), cube(region("ADA", 0, 4 * D), KD)]
        ada0 = [region("CACHE", 0, 4 * D), region("CACHE", 4 * D, 4 * D), region("QK", 0, 4 * D),
                region("ADA", 0, 4 * D)]
        ada0 = [cube(r, 2) for r in ada0]
        ada = ada0[3]
        qT = cube(region("QK", 0, AT * T), AT)
        kT = cube(region("QK", AT * T, AT * T), AT)
        mergedT = cube(region("QK", 0, KD * T), KD)
        sig = cube(region("QK", KD * T, 4 * T), 4)
        h2t = cube(region("QK", KD * T, 2 * D), 2)
        delta_i = region("UC", 0, 512).bitcast(I32)
        low2 = region("UC", 512, 512).bitcast(I32)
        low4 = region("UC", 1024, 512).bitcast(I32)
        delta_f = region("UC", 1536, 512)
        nb1 = region("YC", 512, 512)
        nb2 = region("YC", 1024, 512)
        nb0 = region("YC", 1536, 256)
        EW = 6 * D
        slots = [region("RING", s * EW, EW) for s in range(3)] + [region("VTOK", 0, EW)]
        w_gu = [s[:, 0:4 * D].rearrange("p (k a f) -> p k a f", k=KD, a=2) for s in slots]
        w_dn = [cube(s[:, 4 * D:6 * D], FE) for s in slots]
        rest = layout["CACHE"] + 6 * D + KD * T - layout["RING"] - 3 * EW
        h2T = cube(region("HT", KD * T - rest, D), KD)
        hg = cube(region("ADA", EW - 5 * AW - 2 * T, 2 * D), EUN)
        qk_work = 2 * AT * T - 2928
        ys = cube(region("QK", qk_work, D), 2)
        hTe = cube(region("QK", qk_work + D, D), 2)
        silu = cube(region("QK", qk_work + 2 * D, 2 * P), 2)
        actv = cube(region("QK", qk_work + 2 * D + 2 * P, 2 * P), 2)
        actT = cube(region("QK", qk_work + 2 * D + 4 * P, 2 * P), 2)
        yk = region("RING", 0, 8 * D).rearrange("p (t k d) -> p t k d", t=4, k=2)
        yk_s = region("RING", 8 * D, 2 * D, TS).rearrange("p (k d) -> p k d", k=2)
        gfin_b = region("RING", 10 * D, D)
        mix = cube(region("RING", 11 * D, 2 * D), 2)
        res = cube(region("RING", 13 * D, 2 * D), 2)

        small = [0]

        def take(n, rows=P):
            small[0] += n
            assert small[0] <= 4040, small[0]
            return region("SMALL", small[0] - n, n, rows)

        ident = take(P)
        cvec = cube(take(KD * 32), KD)
        ccT = cube(take(CF * 19), CF)
        gmixT = take(KD)
        qs = take(AW, TS)
        ks = take(AW, TS)
        scS = cube(take(H * 324, TS), H)
        smT = cube(take(G * H * TS), G * H)
        ssq = take(8)
        rstd = take(8)
        minus_half = take(1)
        mx = take(8)
        negm = take(2)
        den = take(2)
        rden = take(2)
        m4 = take(16, TS)
        sc = cube(take(G * H * TS), G)
        wrt = cube(take(KD * 36), KD)
        wk = cube(take(2 * 5), 2)
        rt = [0]

        def rtake(n, rows=P):
            rt[0] += n
            assert rt[0] <= 7 * D
            lo = rt[0] - n
            if lo < 3 * D < rt[0]:
                lo, rt[0] = 4 * D, 4 * D + n
            return region("M", lo, n, rows)

        lgt = cube(rtake(5 * 36), 5)
        rbias = rtake(36)
        iota_e = rtake(NTILE)
        valid = rtake(5)
        tok1 = rtake(5)
        jcol = rtake(1)
        slot_i = rtake(P)
        gmax = rtake(5)
        geq = cube(rtake(5 * 8), 5)
        gidx = rtake(5)
        goh = cube(rtake(5 * 4), 5)
        gexp = cube(rtake(5 * 4), 5)
        ptop = rtake(5)
        prod = rtake(5 * NE).rearrange("p (t g e) -> p t g e", t=5, g=NG)
        sel = cube(rtake(5 * EG), 5)
        vk = cube(rtake(10), 2)
        ik = cube(rtake(10), 2)
        ek = cube(rtake(10), 2)
        ohe = rtake(2 * 5 * NE).rearrange("p (k t e) -> p k t e", k=2, t=5)
        member = cube(rtake(5 * NE), 5)
        upper = rtake(P)
        ones = rtake(P)
        ranks = cube(rtake(5 * NE), 5)
        count = rtake(NE)
        extra = rtake(NE)
        extra_i = rtake(NE).bitcast(I32)
        rank_i = cube(rtake(10).bitcast(I32), 2)
        upto = rtake(NE)
        before = rtake(NE)
        tmp2 = rtake(2 * 5 * NE).rearrange("p (k t e) -> p k t e", k=2, t=5)
        rk = cube(rtake(10), 2)
        bk = cube(rtake(10), 2)
        slotk = cube(rtake(10), 2)
        qk_ = cube(rtake(10), 2)
        tilek = cube(rtake(10), 2)
        code = cube(rtake(10), 2)
        t10 = cube(rtake(10), 2)
        oh_slot = rtake(10 * P).rearrange("p (k t s) -> p k t s", k=2, t=5)
        oh_tile = rtake(10 * NTILE).rearrange("p (k t s) -> p k t s", k=2, t=5)
        oh_val = rtake(10 * 2 * NTILE).rearrange("p (k t s) -> p k t s", k=2, t=5)
        lists_f = rtake(2 * NTILE)
        empty = rtake(2 * NTILE)
        lists = cube(rtake(2 * NTILE).bitcast(I32), 2)
        owner_c = region("M", 8 * D, OVER * NE).rearrange("p (o e) -> p o e", o=OVER)
        owner_f = rtake(OVER)
        owner = rtake(OVER).bitcast(I32)
        nover = rtake(1).bitcast(I32)
        gi = rtake(EUN).bitcast(I32)
        si = rtake(EUN).bitcast(I32)

        ps = [ctx.enter_context(nc.psum_tensor(f"bank{i}", [P, 512], F32)) for i in range(8)]

        q_d = nc.dram_tensor("q_scratch", [TS, AW], F32).ap()
        mod_d = nc.dram_tensor("mod_scratch", [1 + TS, 6 * D], F32).ap()
        h_d = nc.dram_tensor("h_scratch", [2 * T, D // 2], F32).ap()
        y_d = nc.dram_tensor("y_scratch", [4 * T, D // 2], F32).ap()

        s_x = [sem(f"s_xin{i}") for i in range(5)]
        s_c = sem("s_c")
        s_ada = [sem(f"s_ada{i}") for i in range(4)]
        s_win = [sem(f"s_win{i}") for i in range(WRING)]
        s_key = sem("s_key")
        s_val = sem("s_val")
        s_wp = sem("s_wp")
        s_wo = sem("s_wo")
        s_xr = [sem(f"s_xr{i}") for i in range(5)]
        s_e = [sem(f"s_e{i}") for i in range(EUN)]
        s_ident = sem("s_ident")
        s_csilu = sem("s_csilu")
        s_cT = sem("s_cT")
        s_cvec = sem("s_cvec")
        s_adamm = sem("s_adamm")
        s_adaev = sem("s_adaev")
        s_modT = sem("s_modT")
        s_modc = sem("s_modc")
        s_mod = sem("s_mod")
        s_sq = sem("s_sq")
        s_ms = sem("s_ms")
        s_rstd = sem("s_rstd")
        s_xn = sem("s_xn")
        s_xT = sem("s_xT")
        s_hA = sem("s_hA")
        s_hD = sem("s_hD")
        s_half = sem("s_half")
        s_wr = sem("s_wr")
        s_feat = sem("s_feat")
        s_tokT = sem("s_tokT")
        s_tok = sem("s_tok")
        s_bias = sem("s_bias")
        s_kv = sem("s_kv")
        s_modw = sem("s_modw")
        s_modr = sem("s_modr")
        s_qw = sem("s_qw")
        s_qr = sem("s_qr")
        s_kq = sem("s_kq")
        s_kqp = sem("s_kqp")
        s_qk = sem("s_qk")
        s_sread = sem("s_sread")
        s_neg = sem("s_neg")
        s_exp = sem("s_exp")
        s_pT = sem("s_pT")
        s_pA = sem("s_pA")
        s_pD = sem("s_pD")
        s_pv = sem("s_pv")
        s_o = sem("s_o")
        s_smp = sem("s_smp")
        s_self = sem("s_self")
        s_smpv = sem("s_smpv")
        s_smo = sem("s_smo")
        s_u = sem("s_u")
        s_cg = sem("s_cg")
        s_yb = sem("s_yb")
        s_ustw = sem("s_ustw")
        s_sig = sem("s_sig")
        s_proj = sem("s_proj")
        s_mrg = sem("s_mrg")
        s_a2 = sem("s_a2")
        s_wom = sem("s_wom")
        s_x2 = sem("s_x2")
        s_sq2 = sem("s_sq2")
        s_h2 = sem("s_h2")
        s_h2w = [sem(f"s_h2w{i}") for i in range(2)]
        s_h2T = sem("s_h2T")
        s_h2c = sem("s_h2c")
        s_rt = sem("s_rt")
        s_rw = sem("s_rw")
        s_rp = sem("s_rp")
        s_ra = sem("s_ra")
        s_rc = sem("s_rc")
        s_lists = sem("s_lists")
        s_hz = sem("s_hz")
        s_hg = [sem(f"s_hg{i}") for i in range(EUN)]
        s_gx = sem("s_gx")
        s_sx = sem("s_sx")
        s_t = sem("s_t")
        s_te = sem("s_te")
        s_gu = sem("s_gu")
        s_si = sem("s_si")
        s_am = sem("s_am")
        s_ta = sem("s_ta")
        s_at = sem("s_at")
        s_y = sem("s_y")
        s_ye = sem("s_ye")
        s_sc = [sem(f"s_sc{i}") for i in range(2)]
        s_go = sem("s_go")
        s_moe = sem("s_moe")
        s_yk = [sem(f"s_yk{i}") for i in range(5)]
        s_gf = sem("s_gf")
        s_w0 = sem("s_w0")
        s_mix = sem("s_mix")
        s_mixg = sem("s_mixg")
        s_sq3 = sem("s_sq3")
        s_x3 = sem("s_x3")
        s_res = sem("s_res")
        s_out = [sem(f"s_out{i}") for i in range(2)]
        s_dve = sem("s_dve")
        s_pool = sem("s_pool")
        s_act = sem("s_act")

        plan, batches = [], []
        halves = [(n, s) for n in range(NQKV, NEARLY) for s in range(2)]
        hc = [0]

        def more_halves(k, last=NCONV):
            while k and hc[0] < len(halves) and halves[hc[0]][0] < last:
                plan.append(("half", *halves[hc[0]]))
                hc[0] += 1
                k -= 1

        def unit_batches(u):
            b = UNITS[u][0]
            chunks = [(g, lo // P + c) for g, (lo, n) in enumerate(segments(b)) for c in range(n // P)]
            got = []
            for a in range(0, len(chunks), 4):
                got.append(len(batches))
                batches.append(("p", u, a, chunks[a:a + 4], a == 0, a + 4 >= len(chunks)))
            return got

        def turn(u, fill, last):
            got = unit_batches(u)
            plan.append(("turn", got[0]))
            for a, i in enumerate(got):
                if a + 1 < len(got):
                    plan.append(("turn", got[a + 1]))
                if a + 1 == len(got) or a == 0 and len(got) > 2:
                    more_halves(min(fill, 1), last)
                    fill -= 1
                plan.append(("pv", i))

        NU = len(UNITS)
        S_AT = 12

        def no(u):
            return u + (u >= S_AT)

        for s in range(NU + 1):
            late = NEARLY if s >= NU - 1 else NCONV
            if s == S_AT:
                plan.append(("qs",))
            if s < NU:
                plan.append(("qk", s))
            more_halves(1, late)
            if s in (3, 6, 9):
                plan.append(("samples", s // 3 - 1))
            if s >= 1:
                if (s - 1) % H == 0 and s > 1:
                    plan.append(("turn_o", len(batches), (s - 1) // H - 1))
                    batches.append(("o", (s - 1) // H - 1))
                turn(s - 1, 2 if s >= NU - 1 else s % 2, late)
            if s == S_AT + 1:
                plan.append(("turn_s", len(batches)))
                batches.append(("s",))
                plan.append(("pv_s",))
        more_halves(2, NEARLY)
        plan.append(("turn_o", len(batches), NB - 1))
        batches.append(("o", NB - 1))
        more_halves(99, NEARLY)
        plan.append(("turn_u", len(batches)))
        batches.append(("u",))
        pv_after, n_pv = {}, 0
        for i, bt in enumerate(batches):
            n_pv += bt[0] == "p"
            pv_after[i] = n_pv
        NPV = n_pv
        unit_end = {bt[1]: pv_after[i] for i, bt in enumerate(batches) if bt[0] == "p" and bt[5]}

        def width(b):
            return sum(n for _, n in segments(b))

        RB = [(4 if i == 0 else i - 1) for i in range(5)]
        rows = [P, P, P, P, TS]

        kv = (kv0, kv1, kv2)
        p_kv = (p_kv128, p_kv512, p_kv2048)
        s_kvo = (s_kv128, s_kv512, s_kv2048)
        win_v = w_in[0].rearrange("(k p) (t n) -> t p k n", p=P, n=P)
        ada_v = w_ada[0].rearrange("(s k p) (g n) -> g s k p n", k=2, p=P, g=3)
        xp_v = x_prompt[0].rearrange("(t p) d -> t p d", p=P)
        yp_v = y_prompt[0].rearrange("(t p) d -> t p d", p=P)
        xs_v = x_sample.rearrange("b o d -> (b o) d")
        ys_v = y_sample.rearrange("b o d -> (b o) d")
        wg_v = w_gate[0].rearrange("e (j p c) f -> e p j c f", j=2, p=P)
        wu_v = w_up[0].rearrange("e (j p c) f -> e p j c f", j=2, p=P)
        wd_v = w_down[0].rearrange("e (c p) d -> e p c d", p=P)

        def at_least(eng, s, v):
            if not (isinstance(v, int) and v <= 0):
                eng.wait_ge(s, v)

        block = ctx.enter_context(nc.Block())

        @block.sync
        def _(sp):
            sp.dma_start(crow[0:1], c_prompt).then_inc(s_c, 16)
            sp.dma_start(crow[1:1 + TS], c_sample).then_inc(s_c, 16)
            sp.dma_start(ccrow[0:2 * TS], cache_conv[0].rearrange("b j c -> (b j) c")).then_inc(s_c, 16)
            sp.dma_start(ccrow[2 * TS:2 * TS + 3], conv_w[0]).then_inc(s_c, 16)
            sp.dma_start(g8, g_mix.rearrange("o (k p) -> (o k) p", p=P)).then_inc(s_c, 16)
            for j in range(4):
                src = b_ada[0].rearrange("(g j s n) -> j g (s n)", g=3, j=4, s=4)[j:j + 1]
                sp.dma_start(ada_bias[32 * j:32 * j + 32].rearrange("p (g s) n -> p g (s n)", g=3),
                             src.to_broadcast([32, 3, 512])).then_inc(s_c, 16)
            for i in range(5):
                sp.dma_start(x[0:rows[i], i], xp_v[i] if i < 4 else xs_v).then_inc(s_x[i], 16)

            def load_ada(a):
                if a >= 4:
                    sp.wait_ge(s_adamm, a)
                dst = ada0[a] if a < 4 else ada
                for k in range(2):
                    sp.dma_start(dst[:, k], ada_v[a // 4, a % 4, k]).then_inc(s_ada[min(a, 3)], 16)

            for a in range(4):
                load_ada(a)
            for n in range(len(ORDER)):
                if n == 2:
                    sp.wait_ge(s_adamm, 4)
                    for g in range(G):
                        src = kv[g][0].rearrange("b (r s) a h d -> s r a b (h d)", s=DIL[g])[0, :, 0]
                        sp.dma_start(cache[0:KEYS[g], g].rearrange("p (b f) -> p b f", b=TS), src).then_inc(s_key, 16)
                if n % 2 == 0 and 4 <= n // 2 + 2 < 12 and n >= 4:
                    load_ada(n // 2 + 2)
                if n >= WRING:
                    sp.wait_ge(s_half, 2 * (n - WRING + 1))
                sp.dma_start(ring[:, n % WRING], win_v[ORDER[n][1]]).then_inc(s_win[n % WRING], 16)
                if n == NCONV + 1:
                    sp.wait_ge(s_smpv, 1)
                    sp.dma_start(wpa, w_pa[0].rearrange("(c p) n -> p c n", p=P)).then_inc(s_wp, 16)
                    sp.dma_start(wpb, w_pb[0].rearrange("(c p) n -> p c n", p=P)).then_inc(s_wp, 16)
                if n == NCONV + 6:
                    sp.wait_ge(s_pv, NPV)
                    sp.wait_ge(s_adamm, 12)
                    for c in range(2):
                        sp.dma_start(wo[c], w_o[0].rearrange("(k p) n -> p k n", p=P)[:, :, 512 * c:512 * c + 512]
                                     ).then_inc(s_wo, 16)
            sp.dma_start(wrt[:, :, 0:NG], w_rg[0].rearrange("(k p) n -> p k n", p=P)).then_inc(s_wr, 16)
            sp.dma_start(wrt[:, :, NG:NG + NE], w_re[0].rearrange("(k p) n -> p k n", p=P)).then_inc(s_wr, 16)
            sp.wait_ge(s_proj, KD)
            for i in RB:
                sp.dma_start(x[0:rows[i], i], xp_v[i] if i < 4 else xs_v).then_inc(s_xr[i], 16)
            sp.wait_ge(s_mrg, KD)
            sp.wait_ge(s_ustw, 32)

            def load_expert(e, j, se):
                wgu = w_gu[j].rearrange("p (j c) a f -> p j c a f", j=2)
                for src, a in ((wg_v, 0), (wu_v, 1)):
                    s1 = src[e] if isinstance(e, int) else src[bass.ds(e, 1)].rearrange("o p j c f -> (o p) j c f")
                    for jj in range(2):
                        sp.dma_start(wgu[:, jj, :, a], s1[:, jj]).then_inc(se, 16)
                s1 = wd_v[e] if isinstance(e, int) else wd_v[bass.ds(e, 1)].rearrange("o p c d -> (o p) c d")
                sp.dma_start(w_dn[j], s1).then_inc(se, 16)

            for j in range(EUN):
                if j == 3:
                    sp.wait_ge(s_wom, 10)
                load_expert(j, j, s_e[j])
            with sp.Fori(1, NE // EUN) as it:
                for j in range(EUN):
                    sp.wait_ge(s_y, EUN * it + (j + 1 - EUN))
                    load_expert(EUN * it + j, j, s_e[j])
            sp.wait_ge(s_lists, 1)
            n_over = sp.value_load(nover[0:1, 0:1], min_val=0, max_val=OVER)
            with sp.If(n_over > 0):
                with sp.Fori(0, n_over) as o:
                    sp.wait_ge(s_y, o + NE)
                    e = sp.value_load(owner[0:1, bass.ds(o, 1)], min_val=0, max_val=NE - 1)
                    load_expert(e, 0, s_e[0])
            sp.wait_ge(s_moe, 1)
            y4 = y_d.rearrange("(t k j) d -> t k (j d)", k=2, j=2)
            sp.dma_start(gfin_b, g_final.rearrange("(o d) -> o d", o=1).to_broadcast([P, D])).then_inc(s_gf, 16)
            for i in RB:
                if i < 4:
                    sp.dma_start(yk[:, i], y4[i * P:(i + 1) * P]).then_inc(s_yk[i], 16)
                else:
                    sp.dma_start(yk_s, y4[TP:T]).then_inc(s_yk[i], 16)
            for n, i in enumerate(RB):
                sp.wait_ge(s_res, n + 1)
                sp.dma_start(yp_v[i] if i < 4 else ys_v, res[0:rows[i], n % 2]).then_inc(s_out[n % 2], 16)
            sp.wait_ge(s_out[0], 16 * 3)
            sp.wait_ge(s_out[1], 16 * 2)

        @block.gpsimd
        def _(pool):
            own = [0]

            def inverse_root(n, i):
                pool.wait_ge(s_ms, n + 1)
                t = rstd[0:rows[i], i:i + 1]
                pool.tensor_tensor(t, t, minus_half[0:rows[i]], ALU.pow).then_inc(s_rstd, 1)

            def link(ins):
                own[0] += 1
                ins.then_inc(s_pool, 1)
                pool.wait_ge(s_pool, own[0])

            pool.memset(minus_half, -0.5)
            link(pool.memset(ident, 1.0))
            link(pool.affine_select(out=ident, in_=ident, compare_op=ALU.is_equal, fill=0.0, base=0,
                                    pattern=[[-1, P]], channel_multiplier=1))
            pool.engine_nop().then_inc(s_ident, 1)
            pool.iota(delta_i, pattern=[[-1, 512]], base=384, channel_multiplier=1).then_inc(s_bias, 1)
            pool.iota(delta_f, pattern=[[-1, 512]], base=384, channel_multiplier=1,
                      allow_small_or_imprecise_dtypes=True).then_inc(s_bias, 1)
            link(pool.iota(nb0, pattern=[[1, 256]], base=-P, channel_multiplier=-1,
                           allow_small_or_imprecise_dtypes=True))
            link(pool.affine_select(out=nb0, in_=nb0, compare_op=ALU.is_ge, fill=-BIG, base=P,
                                    pattern=[[-1, 256]], channel_multiplier=1))
            link(pool.affine_select(out=nb0, in_=nb0, compare_op=ALU.is_ge, fill=-BIG, base=0,
                                    pattern=[[1, 256]], channel_multiplier=-1))
            for i in range(5):
                inverse_root(i, i)
            pool.wait_ge(s_bias, 4)
            for nb in (nb1, nb2):
                link(pool.affine_select(out=nb, in_=nb, compare_op=ALU.is_ge, fill=-BIG, base=384,
                                        pattern=[[-1, 512]], channel_multiplier=1))
            for h in range(H):
                for g, nb, lo, n in ((0, nb0, 0, 256), (1, nb1, 256, 512), (2, nb2, 768, 512)):
                    ins = pool.tensor_scalar(bias[:, h, lo:lo + n], nb, float(SLOPE[g, h] / SCALE), None, ALU.mult)
            link(ins)
            for f in range(CF):
                link(pool.memset(uT[:, f, 0:2], 0.0))
            pool.engine_nop().then_inc(s_bias, 1)
            pool.wait_ge(s_tok, 2 * AT)
            n_kv = 0
            for g in range(G):
                nt = p_kv[g].shape[2] // P
                for a, (tok, stok) in enumerate(((ktok, ks), (vtok, vtok[0:TS, 4]))):
                    dst = p_kv[g][0, 0].rearrange("(t p) a h d -> p t a (h d)", p=P)[:, :, a]
                    pool.dma_start(dst, tok[:, 4 - nt:4, g * OW:(g + 1) * OW]).then_inc(s_kv, 16)
                    pool.dma_start(s_kvo[g][0, :, 0].rearrange("b a h d -> b a (h d)")[:, a],
                                   stok[:, g * OW:(g + 1) * OW]).then_inc(s_kv, 16)
                    n_kv += 2
            pool.dma_start(s_conv[0, :, 0], cache_conv[0, :, 1]).then_inc(s_kv, 16)
            pool.wait_ge(s_kv, 16 * (n_kv + 1))
            pool.engine_nop().then_inc(s_bias, 1)
            pool.wait_ge(s_adaev, 3)
            for j in range(4):
                dst = mod_d.rearrange("r (g j n) -> j r g n", g=3, j=4)[j][:, 1:3]
                pool.dma_start(dst, mods[32 * j:32 * j + 1 + TS, 4:12].rearrange("p (g s) n -> p g (s n)", g=2)
                               ).then_inc(s_modw, 16)
            pool.wait_ge(s_tok, NQKV)
            pool.dma_start(q_d, qs).then_inc(s_qw, 16)
            pool.wait_ge(s_qw, 16)
            pool.wait_ge(s_modw, 64)
            for g in range(G):
                if g:
                    pool.wait_ge(s_kqp, g)
                pool.dma_start(qb.rearrange("p (b f) -> p b f", b=TS),
                               q_d[:, g * OW:(g + 1) * OW].rearrange("(o b) f -> o b f", o=1)
                               .to_broadcast([P, TS, OW])).then_inc(s_qr, 16)
            for h in range(H):
                for g in range(G):
                    pool.iota(biasS[:, h, g], pattern=[[DIL[g], P]], base=-DIL[g] * KEYS[g], channel_multiplier=0,
                              allow_small_or_imprecise_dtypes=True)
            link(pool.engine_nop())
            for h in range(H):
                for g in range(G):
                    ins = pool.tensor_scalar(biasS[:, h, g], biasS[:, h, g], float(SLOPE[g, h] / SCALE), None, ALU.mult)
            link(ins)
            pool.engine_nop().then_inc(s_bias, 1)
            pool.wait_ge(s_kq, G)
            for g in range(G):
                src = kv[g][0].rearrange("b (r s) a h d -> s r a b (h d)", s=DIL[g])[0, :, 1]
                pool.dma_start(cache[0:KEYS[g], g].rearrange("p (b f) -> p b f", b=TS), src).then_inc(s_val, 16)
            pool.wait_ge(s_sread, G * (NU + 1))
            md = mod_d[:, 2 * D:6 * D].rearrange("r (v d) -> r v d", v=4)
            pool.dma_start(mod_p, md[0:1].to_broadcast([P, 4, D])).then_inc(s_modr, 16)
            pool.dma_start(mod_s, md[1:1 + TS]).then_inc(s_modr, 16)
            pool.dma_start(gffn_b, g_ffn.to_broadcast([P, D])).then_inc(s_modr, 16)
            pool.wait_ge(s_pD if (len(batches) - 1) % 2 else s_pA, (len(batches) - 1) // 2 + 1)
            pool.dma_start(p_conv[0, 0], ustate[0:2]).then_inc(s_ustw, 16)
            pool.dma_start(s_conv[0, :, 1], ustate[2:2 + TS]).then_inc(s_ustw, 16)
            pool.wait_ge(s_ustw, 32)
            for n, i in enumerate(RB):
                inverse_root(5 + n, i)
                pool.wait_ge(s_h2, n + 1)
                dst = h_d.rearrange("(t j) d -> t (j d)", j=2)[i * P:i * P + rows[i]]
                pool.dma_start(dst, h2t[0:rows[i], n % 2]).then_inc(s_h2w[n % 2], 16)
            pool.wait_ge(s_h2, 5)
            f = dict(allow_small_or_imprecise_dtypes=True)
            pool.iota(iota_e, pattern=[[1, NTILE]], base=0, channel_multiplier=0, **f)
            pool.iota(slot_i.rearrange("p (j s) -> p j s", j=2), pattern=[[0, 2], [1, R]], base=0,
                      channel_multiplier=0, **f)
            pool.iota(tok1, pattern=[[P, 5]], base=1, channel_multiplier=1, **f)
            pool.memset(valid, 1.0)
            pool.memset(jcol, 0.0)
            pool.memset(upper, 1.0)
            link(pool.memset(ones, 1.0))
            link(pool.affine_select(out=valid[:, 4:5], in_=valid[:, 4:5], compare_op=ALU.is_ge, fill=0.0, base=TS - 1,
                                    pattern=[[0, 1]], channel_multiplier=-1))
            link(pool.affine_select(out=jcol, in_=jcol, compare_op=ALU.is_ge, fill=1.0, base=R - 1,
                                    pattern=[[0, 1]], channel_multiplier=-1))
            link(pool.affine_select(out=upper, in_=upper, compare_op=ALU.is_gt, fill=0.0, base=0,
                                    pattern=[[1, P]], channel_multiplier=-1))
            link(pool.tensor_tensor(tok1, tok1, valid, ALU.mult))
            pool.dma_start(rbias[:, 0:NG], b_rg.to_broadcast([P, NG])).then_inc(s_rc, 16)
            pool.dma_start(rbias[:, NG:NG + NE], b_re.to_broadcast([P, NE])).then_inc(s_rc, 16)
            pool.wait_ge(s_h2c, 10)
            pool.wait_ge(s_rt, 5)
            link(pool.memset(hg.rearrange("p a b -> p (a b)"), 0.0))
            pool.wait_ge(s_lists, 1)
            pool.wait_ge(s_h2w[0], 48)
            pool.wait_ge(s_h2w[1], 32)
            last_read, last_written = pool.to_reg(2 * T - 1), pool.to_reg(4 * T - 1)

            def apart(s, v):
                if not (isinstance(v, int) and v <= 0):
                    pool.wait_ge(s, v)
                    pool.sem_inc(s_go, 1)

            def gather(e, j, ix):
                apart(s_t, e - EUN + 1)
                pool.tensor_copy(gi[:, j:j + 1], lists[:, 1, ix]).then_inc(s_gx, 1)
                apart(s_gx, e + 1)
                pool.indirect_dma_start(out=hg[:, j], out_offset=None, in_=h_d,
                                        in_offset=bass.IndirectOffsetOnAxis(ap=gi[:, j:j + 1], axis=0),
                                        bounds_check=last_read, oob_is_err=False).then_inc(s_hg[j], 16)

            def scatter(e, j, ix):
                pool.tensor_copy(si[:, j:j + 1], lists[:, 0, ix]).then_inc(s_sx, 1)
                apart(s_sx, e + 1)
                apart(s_ye, e + 1)
                b = j % 2
                pool.indirect_dma_start(out=y_d, out_offset=bass.IndirectOffsetOnAxis(ap=si[:, j:j + 1], axis=0),
                                        in_=ys[:, b], in_offset=None,
                                        bounds_check=last_written, oob_is_err=False).then_inc(s_sc[b], 16)

            def column(e):
                return slice(e, e + 1) if isinstance(e, int) else bass.ds(e, 1)

            def four(it, last=False):
                e0 = EUN * it
                for j in range(EUN):
                    ahead = j + AHEAD
                    if not last or ahead < EUN:
                        gather(e0 + ahead, ahead % EUN, column(e0 + ahead))
                    scatter(e0 + j, j, column(e0 + j))

            for e in range(AHEAD):
                gather(e, e, column(e))
            four(0)
            with pool.Fori(1, NE // EUN - 1) as it:
                four(it)
            four(NE // EUN - 1, True)
            n_over = pool.value_load(nover[0:1, 0:1], min_val=0, max_val=OVER)
            with pool.If(n_over > 0):
                with pool.Fori(0, n_over) as o:
                    apart(s_ye, o + NE)
                    gather(o + NE, 0, bass.ds(o + NE, 1))
                    scatter(o + NE, 0, bass.ds(o + NE, 1))
                    apart(s_sc[0], 16 * o + (16 * (NE // 2) + 16))
            pool.wait_ge(s_sc[0], 16 * (NE // 2))
            pool.wait_ge(s_sc[1], 16 * (NE // 2))
            pool.engine_nop().then_inc(s_moe, 1)
            for n, i in enumerate(RB):
                r = rows[i]
                md = mod_p if i < 4 else mod_s
                pool.wait_ge(s_mix, n + 1)
                pool.tensor_tensor(mix[0:r, n % 2], mix[0:r, n % 2], md[0:r, 3], ALU.mult).then_inc(s_mixg, 1)
                if n:
                    inverse_root(10 + n - 1, RB[n - 1])
            inverse_root(14, RB[4])

        def copy_h2(act, n):
            r = rows[RB[n]]
            for c in range(2):
                act.wait_ge(s_h2T, 2 * n + c + 1)
                if n and c == 0:
                    act.wait_ge(s_rt, n)
                act.activation(h2T[:, 4 * c:4 * c + 4, 0:r],
                               ps[6 + c][:].rearrange("p (k t) -> p k t", k=4)[:, :, 0:r], ACT.Copy).then_inc(s_h2c, 1)

        @block.scalar
        def _(act):
            act.wait_ge(s_c, 16 * 9)
            act.activation(crow, crow, ACT.Silu).then_inc(s_csilu, 1)
            for i in range(5):
                act.wait_ge(s_x[i], 16)
                at_least(act, s_sq, i)
                act.activation(region("HT", 3 * D, D, rows[i]),
                               x[0:rows[i], i], ACT.Square, accum_out=ssq[0:rows[i], i:i + 1]).then_inc(s_sq, 1)
            act.wait_ge(s_mod, 1)
            for k in range(KD):
                act.wait_ge(s_xT, k + 1)
                j, cc = k // 4, k % 4
                act.activation(hT[:, k, 0:TP], ps[2 + 2 * (k % 2)][:], ACT.Identity,
                               bias=modT[:, cc, 32 * j:32 * j + 1], scale=modT[:, cc, 64 + 32 * j:65 + 32 * j]
                               ).then_inc(s_hA, 1)

            def feature(n, s):
                kind, _, f = ORDER[n]
                act.wait_ge(s_half, 2 * n + s + 1)
                src = ps[s][:, 0:HALF]
                span = slice(s * HALF, (s + 1) * HALF)
                if kind in "vkq":
                    if kind == "v" and s == 0:
                        at_least(act, s_tokT, n - 1)
                    dst = {"v": vst[:, n % 2], "k": kT[:, f], "q": qT[:, f]}[kind]
                    act.activation(dst[:, span], src, ACT.Copy).then_inc(s_feat, 1)
                elif kind == "c":
                    if f:
                        act.wait_ge(s_u, 2 * f)
                    act.activation(cgate[:, span], src, ACT.Copy).then_inc(s_cg, 1)
                elif kind in ("ga", "gb"):
                    if n == NCONV and s == 0:
                        act.wait_ge(s_qk, G * (NU + 1))
                    if f >= 2 and s == 0:
                        act.wait_ge(s_mrg, f - 1)
                    dst = sig[:, (0 if kind == "ga" else 2) + f % 2]
                    act.activation(dst[:, span], src, ACT.Sigmoid).then_inc(s_sig, 1)

            for n in range(NQKV):
                for s in range(2):
                    feature(n, s)
            batch = 0
            act.wait_ge(s_bias, 6)
            for what, *a in plan:
                if what == "half":
                    if ORDER[a[0]][0] in ("c", "ga", "gb"):
                        feature(*a)
                elif what == "qk":
                    pass
                elif what == "turn" and a[0] % 2 == 0:
                    i = a[0]
                    nch = len(batches[i][3])
                    act.wait_ge(s_pT, i + 1)
                    at_least(act, s_pv, pv_after[i - 2] if i >= 2 else 0)
                    act.activation(probT[:, 0, 0:nch * P], ps[5][:, 0:nch * P], ACT.Copy).then_inc(s_pA, 1)
                elif what == "turn_o" and a[0] % 2 == 0:
                    act.wait_ge(s_pT, a[0] + 1)
                    act.activation(attnT[:, :, a[1] * P:(a[1] + 1) * P],
                                   ps[5][:, 0:2 * P].rearrange("p (c t) -> p c t", c=2), ACT.Copy).then_inc(s_pA, 1)
                elif what == "turn_s" and a[0] % 2 == 0:
                    act.wait_ge(s_pT, a[0] + 1)
                    flat = smT.rearrange("p a b -> p (a b)")
                    act.activation(flat[:, 0:64], ps[5][:, 0:64], ACT.Copy)
                    act.activation(flat[0:64, 64:96], ps[5][0:64, 64:96], ACT.Copy).then_inc(s_pA, 1)
                elif what == "turn_u" and a[0] % 2 == 0:
                    act.wait_ge(s_pT, a[0] + 1)
                    act.activation(ustate, ps[5][0:2 + TS, :], ACT.Copy).then_inc(s_pA, 1)
                if what == "qk":
                    u = a[0]
                    b = UNITS[u][0]
                    act.wait_ge(s_neg, no(u) + 1)
                    act.activation(prob[:, u % 2, 0:width(b)], prob[:, u % 2, 0:width(b)], ACT.Exp,
                                   bias=negm[:, u % 2:u % 2 + 1], accum_out=den[:, u % 2:u % 2 + 1]
                                   ).then_inc(s_exp, 1)
                elif what == "qs":
                    act.wait_ge(s_neg, S_AT + 1)
                    act.activation(scS[:, :, 0:323], scS[:, :, 0:323], ACT.Exp).then_inc(s_exp, 1)
            for n in range(NEARLY, len(ORDER)):
                for s in range(2):
                    feature(n, s)
            for n, i in enumerate(RB):
                r = rows[i]
                act.wait_ge(s_x2, n + 1)
                act.activation(h2t[0:r, n % 2], x[0:r, i], ACT.Square, accum_out=ssq[0:r, i:i + 1]).then_inc(s_sq2, 1)
                if n:
                    copy_h2(act, n - 1)
            copy_h2(act, 4)
            act.wait_ge(s_rw, 1)
            act.activation(gexp, gexp, ACT.Exp).then_inc(s_ra, 1)
            act.wait_ge(s_rw, 2)
            act.activation(wk[:, 1], wk[:, 1], ACT.Exp).then_inc(s_ra, 1)

            def expert(e, j, last=None):
                b = j % 2
                act.wait_ge(s_t, e + 1)
                at_least(act, s_gu, e - 1)
                act.activation(hTe[:, b], ps[b][:], ACT.Copy).then_inc(s_te, 1)

            def silu_of(e, j):
                b = j % 2
                act.wait_ge(s_gu, e + 1)
                at_least(act, s_am, e - 1)
                act.activation(silu[:, b], ps[2 + b][:, 0:P], ACT.Silu).then_inc(s_si, 1)

            def four(it, last=False):
                e0 = EUN * it
                for j in range(EUN):
                    if not last or j + 1 < EUN:
                        expert(e0 + (j + 1), j + 1)
                    silu_of(e0 + j, j)

            expert(0, 0)
            four(0)
            with act.Fori(1, NE // EUN - 1) as it:
                four(it)
            four(NE // EUN - 1, True)
            act.wait_ge(s_lists, 1)
            n_over = act.value_load(nover[0:1, 0:1], min_val=0, max_val=OVER)
            with act.If(n_over > 0):
                with act.Fori(0, n_over) as o:
                    expert(o + NE, 0)
                    silu_of(o + NE, 0)
            def weigh(n):
                i = RB[n]
                r = rows[i]
                pair = yk[:, i] if i < 4 else yk_s
                act.wait_ge(s_yk[i], 16)
                act.activation(pair[0:r, 0], pair[0:r, 0], ACT.Copy, scale=wk[0:r, 0, i:i + 1]).then_inc(s_w0, 1)

            weigh(0)
            weigh(1)
            for n, i in enumerate(RB):
                r = rows[i]
                if n + 2 < 5:
                    weigh(n + 2)
                act.wait_ge(s_x3, n + 1)
                act.activation(mix[0:r, n % 2], x[0:r, i], ACT.Square, accum_out=ssq[0:r, i:i + 1]).then_inc(s_sq3, 1)

        @block.vector
        def _(dve):
            own = [0]

            def link(ins):
                own[0] += 1
                ins.then_inc(s_dve, 1)
                dve.wait_ge(s_dve, own[0])

            link(dve.memset(cvec.rearrange("p k r -> p (k r)"), 0.0))
            dve.wait_ge(s_bias, 2)
            dve.tensor_scalar(low2, delta_i, DIL[1] - 1, None, ALU.bitwise_and)
            link(dve.tensor_scalar(low4, delta_i, DIL[2] - 1, None, ALU.bitwise_and))
            for nb, low in ((nb1, low2), (nb2, low4)):
                dve.scalar_tensor_tensor(out=nb, in0=low, scalar=-BIG, in1=delta_f, op0=ALU.mult,
                                         op1=ALU.subtract).then_inc(s_bias, 1)
            dve.wait_ge(s_cT, 1)
            dve.tensor_copy(cvec[:, :, 0:1 + TS], cube(ps[2][:, 0:KD * 32], KD)[:, :, 0:1 + TS])
            dve.tensor_copy(ccT, cube(ps[3][:, 0:CF * 32], CF)[:, :, 0:19])
            dve.tensor_copy(gmixT, ps[3][:, CF * 32:CF * 32 + KD]).then_inc(s_cvec, 1)
            for i in range(5):
                r = rows[i]
                dve.wait_ge(s_sq, i + 1)
                dve.tensor_scalar(rstd[0:r, i:i + 1], ssq[0:r, i:i + 1], 1.0 / D, EPS, ALU.mult, ALU.add).then_inc(s_ms, 1)
                dve.wait_ge(s_rstd, i + 1)
                dve.tensor_scalar(x[0:r, i], x[0:r, i], rstd[0:r, i:i + 1], None, ALU.mult).then_inc(s_xn, 1)

            def ada_out(g):
                dve.wait_ge(s_adamm, 4 * g + 4)
                dve.tensor_tensor(mods[:, 4 * g:4 * g + 4], cube(ps[6 + g % 2][:], 4), ada_bias[:, 4 * g:4 * g + 4],
                                  ALU.add).then_inc(s_adaev, 1)

            ada_out(0)
            dve.wait_ge(s_modT, 1)
            link(dve.tensor_copy(modT, cube(ps[0][:], 4)))
            for k in range(KD):
                m = modT[:, k % 4, 64 + 32 * (k // 4):64 + 32 * (k // 4) + 1 + TS]
                ins = dve.tensor_scalar(m, m, 1.0, gmixT[:, k:k + 1], ALU.add, ALU.mult)
            link(ins)
            dve.engine_nop().then_inc(s_mod, 1)
            for k in range(KD):
                dve.wait_ge(s_xT, k + 1)
                j, cc = k // 4, k % 4
                h = hT[:, k, TP:T]
                link(dve.tensor_tensor(h, ps[3 + 2 * (k % 2)][:, 0:TS], modT[:, cc, 65 + 32 * j:65 + 32 * j + TS],
                                       ALU.mult))
                dve.tensor_tensor(h, h, modT[:, cc, 1 + 32 * j:1 + 32 * j + TS], ALU.add).then_inc(s_hD, 1)

            def by_rows(n):
                kind, _, f = ORDER[n]
                dve.wait_ge(s_tokT, n + 1)
                pr, sm = ps[2 + 2 * (n % 2)], ps[3 + 2 * (n % 2)]
                cols = slice(f * P, (f + 1) * P)
                if kind != "q":
                    tok = vtok if kind == "v" else ktok
                    dve.tensor_copy(tok[:, 0:NB, cols], cube(pr[:], NB))
                dst = {"v": vtok[0:TS, NB, cols], "k": ks[:, cols], "q": qs[:, cols]}[kind]
                dve.tensor_copy(dst, sm[0:TS, 0:P]).then_inc(s_tok, 1)

            for n in range(NQKV):
                if n:
                    by_rows(n - 1)
                if n in (9, 17):
                    ada_out((n + 5) // 8)
            by_rows(NQKV - 1)

            def feature(n, s):
                kind, _, f = ORDER[n]
                span = slice(s * HALF, (s + 1) * HALF)
                src = ps[s][:, 0:HALF]
                if kind == "u":
                    dve.wait_ge(s_half, 2 * n + s + 1)
                    dve.wait_ge(s_cg, 2 * f + s + 1)
                    dve.tensor_tensor(uT[:, f, 2 + s * HALF:2 + (s + 1) * HALF], src, cgate[:, span],
                                      ALU.mult).then_inc(s_u, 1)
                    if s == 1:
                        dve.wait_ge(s_u, 2 * f + 2)
                        conv(f)
                elif kind == "b":
                    dve.wait_ge(s_half, 2 * n + s + 1)
                    dve.tensor_tensor(yT[:, f, span], src, yT[:, f, span], ALU.mult).then_inc(s_yb, 1)

            def conv(f):
                tap = [ccT[:, f, 2 * TS + j:2 * TS + j + 1] for j in range(3)]
                for dst, src in ((yT[:, f, 0:TP], [uT[:, f, j:j + TP] for j in range(3)]),
                                 (yT[:, f, TP:T], [ccT[:, f, 0:2 * TS:2], ccT[:, f, 1:2 * TS:2],
                                                   uT[:, f, TP + 2:T + 2]])):
                    link(dve.tensor_scalar(dst, src[0], tap[0], None, ALU.mult))
                    for j in (1, 2):
                        link(dve.scalar_tensor_tensor(out=dst, in0=src[j], scalar=tap[j], in1=dst, op0=ALU.mult,
                                                      op1=ALU.add))

            batch_o = {bt[1]: i for i, bt in enumerate(batches) if bt[0] == "o"}
            last_turn = {}
            for i, bt in enumerate(batches):
                if bt[0] == "p":
                    last_turn[bt[1]] = i
            flatS = scS[:, :, 0:323]
            for what, *a in plan:
                if what == "half":
                    feature(*a)
                elif what == "qk":
                    u = a[0]
                    b, h = UNITS[u]
                    off = 0
                    dve.wait_ge(s_bias, 6)
                    if u >= 2:
                        dve.wait_ge(s_pT, last_turn[u - 2] + 1)
                    for g, (lo, n) in enumerate(segments(b)):
                        dve.wait_ge(s_qk, G * no(u) + g + 1)
                        at_b = lo - P * b + P if g == 0 else 256 + 512 * (g - 1) + 384 - P * b + lo
                        dve.tensor_tensor_reduce(prob[:, u % 2, off:off + n], ps[2 + g][:, 0:n],
                                                 bias[:, h, at_b:at_b + n], SCALE, -3.0e38, ALU.add, ALU.max,
                                                 mx[:, 4 * (u % 2) + g:4 * (u % 2) + g + 1]).then_inc(s_sread, 1)
                        off += n
                    dve.wait_ge(s_sread, G * (no(u) + 1))
                    m = mx[:, 4 * (u % 2) + 3:4 * (u % 2) + 4]
                    link(dve.tensor_reduce(m, mx[:, 4 * (u % 2):4 * (u % 2) + 3], AX.X, ALU.max))
                    if u >= 2:
                        dve.wait_ge(s_exp, no(u - 2) + 1)
                    dve.tensor_scalar(negm[:, u % 2:u % 2 + 1], m, -1.0, None, ALU.mult).then_inc(s_neg, 1)
                elif what == "samples":
                    g = a[0]
                    kr = cache[0:KEYS[g], g]
                    dve.wait_ge(s_key, 16 * G)
                    dve.wait_ge(s_qr, 16 * (g + 1))
                    dve.tensor_tensor(kr, kr, qb[0:KEYS[g]], ALU.mult).then_inc(s_kqp, 1)
                    dve.wait_ge(s_kqp, g + 1)
                    dve.tensor_reduce(sc[0:KEYS[g], g], kr.rearrange("p (a d) -> p a d", d=DH), AX.X,
                                      ALU.add).then_inc(s_kq, 1)
                    if g == 0:
                        link(dve.tensor_tensor(selfp, qs, ks, ALU.mult))
                        link(dve.tensor_reduce(scS[:, :, 320:323].rearrange("p h g -> p g h"),
                                               selfp.rearrange("p (g h d) -> p g h d", g=G, h=H), AX.X, ALU.add))
                elif what == "qs":
                    dve.wait_ge(s_bias, 7)
                    off = 0
                    for g in range(G):
                        dve.wait_ge(s_qk, G * S_AT + g + 1)
                        n = KEYS[g]
                        dve.tensor_tensor(scS[:, :, off:off + n],
                                          ps[2 + g][0:TS, 0:H * n].rearrange("p (h r) -> p h r", h=H),
                                          biasS[:, :, g, 0:n], ALU.add).then_inc(s_sread, 1)
                        off += n
                    dve.wait_ge(s_sread, G * (S_AT + 1))
                    link(dve.tensor_scalar(flatS, flatS, SCALE, None, ALU.mult))
                    link(dve.tensor_reduce(m4[:, 0:4], flatS, AX.X, ALU.max))
                    dve.tensor_tensor(flatS, flatS, m4[:, 0:4].unsqueeze(2).to_broadcast([TS, H, 323]),
                                      ALU.subtract).then_inc(s_neg, 1)
                elif what == "turn" and a[0] % 2 == 1:
                    i = a[0]
                    nch = len(batches[i][3])
                    dve.wait_ge(s_pT, i + 1)
                    at_least(dve, s_pv, pv_after[i - 2] if i >= 2 else 0)
                    dve.tensor_copy(probT[:, 1, 0:nch * P], ps[6][:, 0:nch * P]).then_inc(s_pD, 1)
                elif what == "turn_o" and a[0] % 2 == 1:
                    dve.wait_ge(s_pT, a[0] + 1)
                    dve.tensor_copy(attnT[:, :, a[1] * P:(a[1] + 1) * P],
                                    ps[6][:, 0:2 * P].rearrange("p (c t) -> p c t", c=2)).then_inc(s_pD, 1)
                elif what == "turn_u" and a[0] % 2 == 1:
                    dve.wait_ge(s_pT, a[0] + 1)
                    dve.tensor_copy(ustate, ps[6][0:2 + TS, :]).then_inc(s_pD, 1)
                elif what == "pv" and batches[a[0]][5]:
                    u = batches[a[0]][1]
                    b, h = UNITS[u]
                    dve.wait_ge(s_exp, no(u) + 1)
                    link(dve.reciprocal(rden[:, u % 2:u % 2 + 1], den[:, u % 2:u % 2 + 1]))
                    dve.wait_ge(s_pv, unit_end[u])
                    if h == 0 and b:
                        dve.wait_ge(s_pT, batch_o[b - 1] + 1)
                    dve.tensor_scalar(otok[:, h * DH:(h + 1) * DH], ps[7][:, h * DH:(h + 1) * DH],
                                      rden[:, u % 2:u % 2 + 1], None, ALU.mult).then_inc(s_o, 1)
                if what == "turn_s":
                    dve.wait_ge(s_exp, S_AT + 1)
                    link(dve.tensor_reduce(m4[:, 4:8], flatS, AX.X, ALU.add))
                    link(dve.reciprocal(m4[:, 8:12], m4[:, 4:8]))
                    dve.tensor_tensor(flatS, flatS, m4[:, 8:12].unsqueeze(2).to_broadcast([TS, H, 323]),
                                      ALU.mult).then_inc(s_smp, 1)
                    dve.wait_ge(s_smp, 1)
                    own_p = scS[:, :, 320:323].rearrange("p h g -> p g h").unsqueeze(3).to_broadcast([TS, G, H, DH])
                    link(dve.tensor_tensor(selfp.rearrange("p (g h d) -> p g h d", g=G, h=H),
                                           vtok[0:TS, NB].rearrange("p (g h d) -> p g h d", g=G, h=H), own_p,
                                           ALU.mult))
                    dve.tensor_reduce(selfs, selfp.rearrange("p (g f) -> p f g", g=G), AX.X, ALU.add
                                      ).then_inc(s_self, 1)
                    if a[0] % 2 == 1:
                        dve.wait_ge(s_pT, a[0] + 1)
                        flat = smT.rearrange("p a b -> p (a b)")
                        dve.tensor_copy(flat[:, 0:64], ps[6][:, 0:64])
                        dve.tensor_copy(flat[0:64, 64:96], ps[6][0:64, 64:96]).then_inc(s_pD, 1)
                elif what == "pv_s":
                    dve.wait_ge(s_smpv, 1)
                    dve.tensor_copy(attnT[:, :, TP:T], ps[7][:, 256:256 + 2 * TS].rearrange("p (c b) -> p c b", c=2)
                                    ).then_inc(s_smo, 1)
            for f in range(KD):
                dve.wait_ge(s_sig, 4 * f + 4)
                dve.wait_ge(s_proj, f + 1)
                for s in range(2):
                    span = slice(s * HALF, (s + 1) * HALF)
                    sa, sb_ = sig[:, f % 2, span], sig[:, 2 + f % 2, span]
                    dve.tensor_tensor(sa, ps[2 + s][:, 0:HALF], sa, ALU.mult)
                    ins = dve.tensor_tensor(sb_, ps[4 + s][:, 0:HALF], sb_, ALU.mult)
                link(ins)
                dve.tensor_tensor(mergedT[:, f], sig[:, f % 2], sig[:, 2 + f % 2], ALU.add).then_inc(s_mrg, 1)
            dve.wait_ge(s_modr, 48)
            link(dve.tensor_scalar(mod_p[:, 2], mod_p[:, 2], 1.0, None, ALU.add))
            link(dve.tensor_tensor(mod_p[:, 2], mod_p[:, 2], gffn_b, ALU.mult))
            link(dve.tensor_scalar(mod_s[:, 2], mod_s[:, 2], 1.0, None, ALU.add))
            link(dve.tensor_tensor(mod_s[:, 2], mod_s[:, 2], gffn_b[0:TS], ALU.mult))
            for n, i in enumerate(RB):
                r = rows[i]
                md = mod_p if i < 4 else mod_s
                h2 = h2t[0:r, n % 2]
                if n >= 2:
                    dve.wait_ge(s_h2w[n % 2], 16 * (n // 2))
                    dve.wait_ge(s_h2T, 2 * (n - 1))
                if n == 0:
                    dve.wait_ge(s_mrg, KD)
                for c in range(2):
                    half = slice(512 * c, 512 * (c + 1))
                    dve.wait_ge(s_wom, 2 * n + c + 1)
                    link(dve.tensor_tensor(h2[:, half], ps[2 + 2 * (n % 2) + c][0:r], md[0:r, 0, half], ALU.mult))
                dve.wait_ge(s_xr[i], 16)
                dve.tensor_tensor(x[0:r, i], x[0:r, i], h2, ALU.add).then_inc(s_x2, 1)
                dve.wait_ge(s_sq2, n + 1)
                dve.tensor_scalar(rstd[0:r, i:i + 1], ssq[0:r, i:i + 1], 1.0 / D, EPS, ALU.mult, ALU.add).then_inc(s_ms, 1)
                dve.wait_ge(s_rstd, 5 + n + 1)
                link(dve.scalar_tensor_tensor(out=h2, in0=x[0:r, i], scalar=rstd[0:r, i:i + 1], in1=md[0:r, 2],
                                              op0=ALU.mult, op1=ALU.mult))
                dve.tensor_tensor(h2, h2, md[0:r, 1], ALU.add).then_inc(s_h2, 1)

            def wide(ap, n):
                return ap.unsqueeze(len(ap.shape)).to_broadcast([*ap.shape, n])

            dve.wait_ge(s_h2, 5)
            link(dve.memset(lgt.rearrange("p t e -> p (t e)"), 0.0))
            dve.wait_ge(s_rt, 5)
            dve.wait_ge(s_rc, 32)
            for n, i in enumerate(RB):
                r = rows[i]
                ins = dve.tensor_tensor(lgt[0:r, i], ps[0][0:r, 64 * n:64 * n + 36], rbias[0:r], ALU.add)
            link(ins)
            lg, le = lgt[:, :, 0:NG], lgt[:, :, NG:NG + NE].rearrange("p t (g e) -> p t g e", g=NG)

            def first_of(dst, vals, top, n):
                eq = geq[:, :, 0:n]
                link(dve.tensor_tensor(eq, vals, wide(top, n), ALU.is_equal))
                link(dve.tensor_scalar(eq, eq, -64.0, None, ALU.mult))
                link(dve.tensor_tensor(eq, eq, iota_e[:, 0:n].unsqueeze(1).to_broadcast([P, 5, n]), ALU.add))
                link(dve.tensor_reduce(dst, eq, AX.X, ALU.min))
                link(dve.tensor_scalar(dst, dst, 64.0, None, ALU.add))

            link(dve.tensor_reduce(gmax, lg, AX.X, ALU.max))
            dve.tensor_tensor(gexp, lg, wide(gmax, NG), ALU.subtract).then_inc(s_rw, 1)
            first_of(gidx, lg, gmax, NG)
            link(dve.tensor_tensor(goh, iota_e[:, 0:NG].unsqueeze(1).to_broadcast([P, 5, NG]), wide(gidx, NG),
                                   ALU.is_equal))
            for i in range(5):
                ins = dve.tensor_tensor(prod[:, i], le[:, i], wide(goh[:, i], EG), ALU.mult)
            link(ins)
            link(dve.tensor_reduce(sel, prod.rearrange("p t g e -> p t e g"), AX.X, ALU.add))
            link(dve.tensor_reduce(vk[:, 0], sel, AX.X, ALU.max))
            first_of(ik[:, 0], sel, vk[:, 0], EG)
            link(dve.tensor_tensor(geq, iota_e[:, 0:EG].unsqueeze(1).to_broadcast([P, 5, EG]), wide(ik[:, 0], EG),
                                   ALU.is_equal))
            link(dve.scalar_tensor_tensor(out=sel, in0=geq, scalar=-BIG, in1=sel, op0=ALU.mult, op1=ALU.add))
            link(dve.tensor_reduce(vk[:, 1], sel, AX.X, ALU.max))
            first_of(ik[:, 1], sel, vk[:, 1], EG)
            dve.tensor_tensor(wk[:, 1], vk[:, 1], vk[:, 0], ALU.subtract).then_inc(s_rw, 1)
            for k in range(2):
                link(dve.scalar_tensor_tensor(out=ek[:, k], in0=gidx, scalar=float(EG), in1=ik[:, k], op0=ALU.mult,
                                              op1=ALU.add))
            for k in range(2):
                link(dve.tensor_tensor(ohe[:, k], iota_e[:, 0:NE].unsqueeze(1).to_broadcast([P, 5, NE]),
                                       wide(ek[:, k], NE), ALU.is_equal))
            link(dve.tensor_tensor(member, ohe[:, 0], ohe[:, 1], ALU.add))
            dve.tensor_tensor(member, member, wide(valid, NE), ALU.mult).then_inc(s_rw, 1)
            dve.wait_ge(s_ra, 2)
            link(dve.tensor_reduce(ptop, gexp, AX.X, ALU.add))
            link(dve.scalar_tensor_tensor(out=wk[:, 0], in0=wk[:, 1], scalar=1.0, in1=ptop, op0=ALU.add,
                                          op1=ALU.mult))
            link(dve.reciprocal(wk[:, 0], wk[:, 0]))
            link(dve.tensor_tensor(wk[:, 1], wk[:, 1], wk[:, 0], ALU.mult))
            dve.wait_ge(s_rp, 1)
            dve.tensor_copy(ranks, cube(ps[2][:, 0:5 * NE], 5))
            link(dve.tensor_copy(count, ps[2][:, 5 * NE:6 * NE]))
            link(dve.tensor_scalar(extra_i, count, float(R - 1), None, ALU.add))
            link(dve.tensor_scalar(extra_i, extra_i, RBITS, None, ALU.arith_shift_right))
            link(dve.tensor_scalar(extra, extra_i, -1.0, None, ALU.add))
            link(dve.tensor_scalar(extra, extra, 0.0, None, ALU.max))
            link(dve.tensor_tensor_scan(upto, extra, extra, 0.0, ALU.add, ALU.bypass))
            link(dve.tensor_tensor(before, upto, extra, ALU.subtract))
            for k in range(2):
                link(dve.tensor_tensor(tmp2[:, k], ohe[:, k], ranks, ALU.mult))
            link(dve.tensor_reduce(rk, tmp2, AX.X, ALU.add))
            for k in range(2):
                link(dve.tensor_tensor(tmp2[:, k], ohe[:, k], before.unsqueeze(1).to_broadcast([P, 5, NE]), ALU.mult))
            link(dve.tensor_reduce(bk, tmp2, AX.X, ALU.add))
            link(dve.tensor_copy(rank_i, rk))
            link(dve.tensor_scalar(rank_i, rank_i, R - 1, None, ALU.bitwise_and))
            link(dve.tensor_copy(slotk, rank_i))
            link(dve.tensor_tensor(qk_, rk, slotk, ALU.subtract))
            link(dve.tensor_scalar(qk_, qk_, 1.0 / R, None, ALU.mult))
            link(dve.tensor_tensor(tilek, bk, qk_, ALU.add))
            link(dve.tensor_scalar(tilek, tilek, float(NE - 1), None, ALU.add))
            link(dve.tensor_tensor(tilek, tilek, ek, ALU.subtract))
            link(dve.tensor_scalar(t10, qk_, 0.5, None, ALU.is_gt))
            link(dve.tensor_tensor(tilek, tilek, t10, ALU.mult))
            link(dve.tensor_tensor(tilek, tilek, ek, ALU.add))
            for k in range(2):
                link(dve.tensor_scalar(code[:, k], tok1, 2.0, float(k - 1), ALU.mult, ALU.add))
                link(dve.tensor_tensor(code[:, k], code[:, k], valid, ALU.mult))
            for k in range(2):
                for i in range(5):
                    dve.tensor_scalar(oh_slot[:, k, i], slot_i, slotk[:, k, i:i + 1], None, ALU.is_equal)
                    ins = dve.tensor_scalar(oh_tile[:, k, i], iota_e, tilek[:, k, i:i + 1], None, ALU.is_equal)
                link(ins)
                for i in range(5):
                    dve.tensor_scalar(oh_val[:, k, i, 0:NTILE], oh_tile[:, k, i], code[:, k, i:i + 1], None, ALU.mult)
                    ins = dve.tensor_scalar(oh_val[:, k, i, NTILE:2 * NTILE], oh_tile[:, k, i], tok1[:, i:i + 1],
                                            None, ALU.mult)
            ins.then_inc(s_rw, 1)
            link(dve.tensor_tensor(owner_c[0:1], upto[0:1].unsqueeze(1).to_broadcast([1, OVER, NE]),
                                   iota_e[0:1, 0:OVER].unsqueeze(2).to_broadcast([1, OVER, NE]), ALU.is_le))
            link(dve.tensor_reduce(owner_f[0:1], owner_c[0:1], AX.X, ALU.add))
            link(dve.tensor_scalar(owner_f[0:1], owner_f[0:1], float(NE - 1), None, ALU.min))
            dve.tensor_copy(owner[0:1], owner_f[0:1])
            link(dve.tensor_copy(nover[0:1], upto[0:1, NE - 1:NE]))
            dve.wait_ge(s_rp, 2)
            link(dve.tensor_copy(lists_f, ps[3][:, 0:2 * NTILE]))
            link(dve.tensor_scalar(empty, lists_f, 0.0, SKIP, ALU.is_equal, ALU.mult))
            link(dve.scalar_tensor_tensor(out=lists_f, in0=lists_f, scalar=2.0, in1=empty, op0=ALU.mult, op1=ALU.add))
            link(dve.tensor_scalar(lists_f, lists_f, -2.0, jcol, ALU.add, ALU.add))
            dve.tensor_copy(lists.rearrange("p a b -> p (a b)"), lists_f).then_inc(s_lists, 1)

            def act_of(e, j):
                b = j % 2
                dve.wait_ge(s_si, e + 1)
                at_least(dve, s_ta, e - 1)
                dve.tensor_tensor(actv[:, b], ps[2 + b][:, P:2 * P], silu[:, b], ALU.mult).then_inc(s_am, 1)

            def act_turned(e, j):
                b = j % 2
                dve.wait_ge(s_ta, e + 1)
                at_least(dve, s_y, e - 1)
                dve.tensor_copy(actT[:, b], ps[4][:, 0:P]).then_inc(s_at, 1)

            def down_of(e, j, written):
                b = j % 2
                dve.wait_ge(s_y, e + 1)
                at_least(dve, s_sc[b], written)
                dve.tensor_copy(ys[:, b], ps[5 + b][:]).then_inc(s_ye, 1)

            def four(it):
                e0 = EUN * it
                for j in range(EUN):
                    act_of(e0 + j, j)
                    if j or not isinstance(it, int) or it:
                        down_of(e0 + (j - 1), j - 1, 8 * e0 + 16 * ((j - 1) // 2))
                    act_turned(e0 + j, j)

            four(0)
            with dve.Fori(1, NE // EUN) as it:
                four(it)
            down_of(NE - 1, NE - 1, 8 * NE - 16)
            n_over = dve.value_load(nover[0:1, 0:1], min_val=0, max_val=OVER)
            with dve.If(n_over > 0):
                with dve.Fori(0, n_over) as o:
                    act_of(o + NE, 0)
                    act_turned(o + NE, 0)
                    down_of(o + NE, 0, 16 * o + 16 * (NE // 2))
            def mixed(n):
                i = RB[n]
                r = rows[i]
                pair = yk[:, i] if i < 4 else yk_s
                dve.wait_ge(s_w0, n + 1)
                if n >= 2:
                    dve.wait_ge(s_sq3, n - 1)
                dve.scalar_tensor_tensor(out=mix[0:r, n % 2], in0=pair[0:r, 1], scalar=wk[0:r, 1, i:i + 1],
                                         in1=pair[0:r, 0], op0=ALU.mult, op1=ALU.add).then_inc(s_mix, 1)

            def summed(n):
                i = RB[n]
                r = rows[i]
                dve.wait_ge(s_mixg, n + 1)
                dve.tensor_tensor(x[0:r, i], x[0:r, i], mix[0:r, n % 2], ALU.add).then_inc(s_x3, 1)

            def mean_square(n):
                i = RB[n]
                r = rows[i]
                dve.wait_ge(s_sq3, n + 1)
                dve.tensor_scalar(rstd[0:r, i:i + 1], ssq[0:r, i:i + 1], 1.0 / D, EPS, ALU.mult, ALU.add
                                  ).then_inc(s_ms, 1)

            def normed(n):
                i = RB[n]
                r = rows[i]
                dve.wait_ge(s_rstd, 10 + n + 1)
                dve.wait_ge(s_gf, 16)
                if n >= 2:
                    dve.wait_ge(s_out[n % 2], 16 * (n // 2))
                dve.scalar_tensor_tensor(out=res[0:r, n % 2], in0=x[0:r, i], scalar=rstd[0:r, i:i + 1],
                                         in1=gfin_b[0:r], op0=ALU.mult, op1=ALU.mult).then_inc(s_res, 1)

            mixed(0)
            for n in range(5):
                if n + 1 < 5:
                    mixed(n + 1)
                if n:
                    mean_square(n - 1)
                summed(n)
                if n:
                    normed(n - 1)
            mean_square(4)
            normed(4)

        @block.tensor
        def _(pe):
            pe.wait_ge(s_ident, 1)
            pe.wait_ge(s_csilu, 1)
            idn = ident
            for k in range(KD):
                pe.transpose(ps[2][:, 32 * k:32 * k + 1 + TS], crow[:, k * P:(k + 1) * P], idn[0:1 + TS, 0:1 + TS])
            for f in range(CF):
                pe.transpose(ps[3][:, 32 * f:32 * f + 19], ccrow[:, f * P:(f + 1) * P], idn[0:19, 0:19])
            pe.transpose(ps[3][:, 32 * CF:32 * CF + KD], g8, idn[0:KD, 0:KD]).then_inc(s_cT, 1)
            pe.wait_ge(s_cvec, 1)

            def ada_step(a):
                w = ada0[a] if a < 4 else ada
                pe.wait_ge(s_ada[min(a, 3)], 32 * (1 + max(0, a - 3)))
                g, first = a // 4, 2 * (a % 4)
                if first == 0:
                    at_least(pe, s_adaev, g - 1)
                for k in (first, first + 1):
                    for j in range(4):
                        ins = pe.matmul(ps[6 + g % 2][32 * j:32 * j + 32, :], cvec[:, k],
                                        w[:, k - first, 512 * j:512 * j + 512],
                                        start=(k == 0), stop=(k == KD - 1), skip_group_check=True)
                ins.then_inc(s_adamm, 1)

            for a in range(4):
                ada_step(a)
            pe.wait_ge(s_adaev, 1)
            for cc in range(4):
                ins = pe.transpose(ps[0][:, cc * P:(cc + 1) * P], mods[:, cc], idn)
            ins.then_inc(s_modT, 1)
            pe.wait_ge(s_xn, 5)
            for k in range(KD):
                at_least(pe, s_hA, k - 1)
                at_least(pe, s_hD, k - 1)
                for i in range(5):
                    r = rows[i]
                    dst = ps[2 + 2 * (k % 2)][:, i * P:(i + 1) * P] if i < 4 else ps[3 + 2 * (k % 2)][:, 0:TS]
                    ins = pe.transpose(dst, x[0:r, i, k * P:(k + 1) * P], idn[0:r, 0:r])
                ins.then_inc(s_xT, 1)
            pe.wait_ge(s_hA, KD)
            pe.wait_ge(s_hD, KD)

            def tile_read(n, s):
                kind, _, f = ORDER[n]
                if kind in "vkq":
                    pe.wait_ge(s_feat, 2 * n + s + 1)
                elif kind == "c":
                    pe.wait_ge(s_cg, 2 * f + s + 1)
                elif kind == "u":
                    pe.wait_ge(s_u, 2 * f + s + 1)
                elif kind == "b":
                    pe.wait_ge(s_yb, 2 * f + s + 1)
                else:
                    pe.wait_ge(s_sig, 2 * (n - NCONV) + s + 1)

            def half(n, s):
                pe.wait_ge(s_win[n % WRING], 16 * (n // WRING + 1))
                if n:
                    tile_read(n - 1, s)
                for k in range(KD):
                    ins = pe.matmul(ps[s][:, 0:HALF], ring[:, n % WRING, k], hT[:, k, s * HALF:(s + 1) * HALF],
                                    start=(k == 0), stop=(k == KD - 1))
                ins.then_inc(s_half, 1)

            def to_rows(n):
                kind, _, f = ORDER[n]
                pe.wait_ge(s_feat, 2 * n + 2)
                at_least(pe, s_tok, n - 1)
                src = {"v": vst[:, n % 2], "k": kT[:, f], "q": qT[:, f]}[kind]
                if kind != "q":
                    for b in range(NB):
                        pe.transpose(ps[2 + 2 * (n % 2)][:, b * P:(b + 1) * P], src[:, b * P:(b + 1) * P], idn)
                pe.transpose(ps[3 + 2 * (n % 2)][0:TS, 0:P], src[:, TP:T], idn).then_inc(s_tokT, 1)

            for n in range(NQKV):
                for s in range(2):
                    half(n, s)
                if n:
                    to_rows(n - 1)
                if n % 2 == 1 and 4 <= (n + 5) // 2 < 12:
                    ada_step((n + 5) // 2)
            to_rows(NQKV - 1)
            pe.wait_ge(s_tok, NQKV)

            for what, *a in plan:
                if what == "half":
                    half(*a)
                elif what == "qk":
                    u = a[0]
                    b, h = UNITS[u]
                    for g, (lo, n) in enumerate(segments(b)):
                        at_least(pe, s_sread, G * (no(u) - 1) + g + 1)
                        f, p0 = 2 * g + h // 2, DH * (h % 2)
                        pe.matmul(ps[2 + g][:, 0:n], qT[p0:p0 + DH, f, b * P:(b + 1) * P], kT[p0:p0 + DH, f, lo:lo + n],
                                  start=True, stop=True).then_inc(s_qk, 1)
                elif what == "qs":
                    pe.wait_ge(s_kq, G)
                    for g in range(G):
                        n = KEYS[g]
                        pe.wait_ge(s_sread, G * (S_AT - 1) + g + 1)
                        for h in range(H):
                            ins = pe.transpose(ps[2 + g][0:TS, h * n:(h + 1) * n], sc[0:n, g, h::H], idn[0:n, 0:n])
                        ins.then_inc(s_qk, 1)
                elif what.startswith("turn"):
                    i = a[0]
                    at_least(pe, s_pD if i % 2 else s_pA, i // 2)
                    bank = ps[5 + i % 2]
                    bt = batches[i]
                    if what == "turn":
                        _, u, first, chunks, _, _ = bt
                        pe.wait_ge(s_exp, no(u) + 1)
                        for c in range(len(chunks)):
                            ins = pe.transpose(bank[:, c * P:(c + 1) * P],
                                               prob[:, u % 2, (first + c) * P:(first + c + 1) * P], idn)
                    elif what == "turn_o":
                        pe.wait_ge(s_o, H * (bt[1] + 1))
                        for c in range(2):
                            ins = pe.transpose(bank[:, c * P:(c + 1) * P], otok[:, c * P:(c + 1) * P], idn)
                    elif what == "turn_s":
                        pe.wait_ge(s_smp, 1)
                        off = 0
                        for g in range(G):
                            n = KEYS[g]
                            for h in range(H):
                                ins = pe.transpose(bank[0:n, (g * H + h) * TS:(g * H + h + 1) * TS],
                                                   scS[:, h, off:off + n], idn[0:TS, 0:TS])
                            off += n
                    else:
                        pe.wait_ge(s_u, 2 * CF)
                        for f in range(CF):
                            ins = pe.transpose(bank[0:2 + TS, f * P:(f + 1) * P], uT[:, f, TP:T + 2], idn)
                    ins.then_inc(s_pT, 1)
                elif what == "pv":
                    i = a[0]
                    _, u, first, chunks, is_first, is_last = batches[i]
                    b, h = UNITS[u]
                    pe.wait_ge(s_pD if i % 2 else s_pA, i // 2 + 1)
                    if is_first:
                        at_least(pe, s_o, u - H + 1)
                    for c, (g, kb) in enumerate(chunks):
                        ins = pe.matmul(ps[7][:, h * DH:(h + 1) * DH], probT[:, i % 2, c * P:(c + 1) * P],
                                        vtok[:, kb, g * OW + h * DH:g * OW + (h + 1) * DH],
                                        start=(is_first and c == 0), stop=(is_last and c == len(chunks) - 1),
                                        skip_group_check=True)
                    ins.then_inc(s_pv, 1)
                elif what == "pv_s":
                    i = [m for m, bt in enumerate(batches) if bt[0] == "s"][0]
                    pe.wait_ge(s_pD if i % 2 else s_pA, i // 2 + 1)
                    pe.wait_ge(s_self, 1)
                    pe.wait_ge(s_val, 16 * G)
                    for c in range(2):
                        pe.matmul(ps[7][:, 256 + c * TS:256 + (c + 1) * TS], selfs[:, c * P:(c + 1) * P],
                                  idn[0:TS, 0:TS], start=(c == 0), stop=False, skip_group_check=True)
                    for g in range(G):
                        n = KEYS[g]
                        val = cache[0:n, g].rearrange("p (b h d) -> p b h d", b=TS, h=H)
                        for h in range(H):
                            c, p0 = h // 2, DH * (h % 2)
                            for b in range(TS):
                                ins = pe.matmul(ps[7][p0:p0 + DH, 256 + c * TS + b:256 + c * TS + b + 1],
                                                val[:, b, h], smT[0:n, g * H + h, b:b + 1], start=False,
                                                stop=(g == G - 1), skip_group_check=True)
                    ins.then_inc(s_smpv, 1)

            pe.wait_ge(s_wp, 32)
            pe.wait_ge(s_smo, 1)
            n_b = len(batches)
            pe.wait_ge(s_pA, (n_b + 1) // 2)
            pe.wait_ge(s_pD, n_b // 2)
            for f in range(KD):
                for n in (NCONV + 2 * f, NCONV + 2 * f + 1):
                    if n >= NEARLY:
                        for s in range(2):
                            half(n, s)
                if f:
                    pe.wait_ge(s_mrg, f)
                for s in range(2):
                    span = slice(s * HALF, (s + 1) * HALF)
                    for c in range(2):
                        pe.matmul(ps[2 + s][:, 0:HALF], wpa[:, c, f * P:(f + 1) * P], attnT[:, c, span],
                                  start=(c == 0), stop=(c == 1))
                    for c in range(CF):
                        ins = pe.matmul(ps[4 + s][:, 0:HALF], wpb[:, c, f * P:(f + 1) * P], yT[:, c, span],
                                        start=(c == 0), stop=(c == CF - 1))
                ins.then_inc(s_proj, 1)
            pe.wait_ge(s_mrg, KD)
            pe.wait_ge(s_wo, 32)

            def router(n):
                r = rows[RB[n]]
                pe.wait_ge(s_h2, n + 1)
                for c in range(2):
                    at_least(pe, s_h2c, 2 * (n - 1) + c + 1)
                    for k in range(4):
                        ins = pe.transpose(ps[6 + c][:, k * P:k * P + r],
                                           h2t[0:r, n % 2, (4 * c + k) * P:(4 * c + k + 1) * P], idn[0:r, 0:r])
                    ins.then_inc(s_h2T, 1)
                pe.wait_ge(s_h2c, 2 * n + 2)
                for k in range(KD):
                    ins = pe.matmul(ps[0][0:r, 64 * n:64 * n + 36], h2T[:, k, 0:r], wrt[:, k], start=(k == 0),
                                    stop=(k == KD - 1), skip_group_check=True)
                ins.then_inc(s_rt, 1)

            pe.wait_ge(s_wr, 32)
            for n, i in enumerate(RB):
                r = rows[i]
                at_least(pe, s_x2, n - 1)
                for c in range(2):
                    for k in range(KD):
                        ins = pe.matmul(ps[2 + 2 * (n % 2) + c][0:r], mergedT[:, k, i * P:i * P + r], wo[c][:, k],
                                        start=(k == 0), stop=(k == KD - 1))
                    ins.then_inc(s_wom, 1)
                if n:
                    router(n - 1)
            router(4)
            pe.wait_ge(s_rw, 3)
            first = True
            for i in range(6):
                for m in range(min(i + 1, 5)):
                    lhs = upper if m == i else ones
                    ins = pe.matmul(ps[2][:, i * NE:(i + 1) * NE], lhs, member[:, m], start=first,
                                    stop=(m == min(i, 4)), skip_group_check=True)
                    first = False
            ins.then_inc(s_rp, 1)
            pe.wait_ge(s_rw, 4)
            for k in range(2):
                for i in range(5):
                    ins = pe.matmul(ps[3][:, 0:2 * NTILE], oh_slot[:, k, i], oh_val[:, k, i], start=(k == 0 and i == 0),
                                    stop=(k == 1 and i == 4))
            ins.then_inc(s_rp, 1)
            pe.wait_ge(s_lists, 1)

            def turn_rows(e, j, gathered):
                b = j % 2
                pe.wait_ge(s_hg[j % EUN], gathered)
                at_least(pe, s_te, e - 1)
                for c in range(4):
                    ins = pe.transpose(ps[b][:, c * P:(c + 1) * P], hg[:, j % EUN, c::4], idn)
                ins.then_inc(s_t, 1)

            def gate_up(e, j, slot, loaded):
                b = j % 2
                pe.wait_ge(s_te, e + 1)
                pe.wait_ge(s_e[slot], loaded)
                at_least(pe, s_am, e - 1)
                for jj in range(2):
                    for c in range(4):
                        for hh in range(2):
                            ins = pe.matmul(ps[2 + b][R * hh:R * hh + R, 0:2 * P],
                                            hTe[:, b, c * P + jj * R:c * P + jj * R + R],
                                            w_gu[slot][:, 4 * jj + c, :, hh * P:(hh + 1) * P],
                                            start=(jj == 0 and c == 0), stop=(jj == 1 and c == 3),
                                            skip_group_check=True)
                ins.then_inc(s_gu, 1)

            def turn_act(e, j):
                pe.wait_ge(s_am, e + 1)
                at_least(pe, s_at, e)
                pe.transpose(ps[4][:, 0:P], actv[:, j % 2], idn).then_inc(s_ta, 1)

            def down(e, j, slot):
                b = j % 2
                pe.wait_ge(s_at, e + 1)
                at_least(pe, s_ye, e - 1)
                for hh in range(2):
                    for jj in range(2):
                        ins = pe.matmul(ps[5 + b][R * jj:R * jj + R], actT[:, b, hh * R:hh * R + R],
                                        w_dn[slot][:, hh, 512 * jj:512 * jj + 512], start=(hh == 0), stop=(hh == 1),
                                        skip_group_check=True)
                ins.then_inc(s_y, 1)

            def four(it, last=False):
                e0 = EUN * it
                for j in range(EUN):
                    if not last or j + 1 < EUN:
                        turn_rows(e0 + (j + 1), j + 1, 16 * it + 16 * ((j + 1) // EUN + 1))
                    gate_up(e0 + j, j, j, 80 * (it + 1))
                    if j or not isinstance(it, int) or it:
                        down(e0 + (j - 1), j - 1, (j - 1) % EUN)
                    turn_act(e0 + j, j)

            turn_rows(0, 0, 16)
            four(0)
            with pe.Fori(1, NE // EUN - 1) as it:
                four(it)
            four(NE // EUN - 1, True)
            down(NE - 1, NE - 1, EUN - 1)
            n_over = pe.value_load(nover[0:1, 0:1], min_val=0, max_val=OVER)
            with pe.If(n_over > 0):
                with pe.Fori(0, n_over) as o:
                    turn_rows(o + NE, 0, 16 * o + (16 * (NE // EUN) + 16))
                    gate_up(o + NE, 0, 0, 80 * o + (80 * (NE // EUN) + 80))
                    turn_act(o + NE, 0)
                    down(o + NE, 0, 0)


_INS = ["x_prompt", "x_sample", "cache_kv_w128", "cache_kv_w512", "cache_kv_w2048", "cache_conv", "c_prompt",
        "c_sample", "g_mix", "w_ada", "b_ada", "w_in", "conv_w", "w_pa", "w_pb", "w_o", "g_ffn", "w_router_group",
        "b_router_group", "w_router_expert", "b_router_expert", "w_gate_e", "w_up_e", "w_down_e", "g_final"]
_OUTS = [(1, TP, D), (TS, 1, D), (1, 1, 128, 2, H, DH), (1, 1, 512, 2, H, DH), (1, 1, 512, 2, H, DH),
         (1, 1, 2, CW), (1, TS, 1, 2, H, DH), (1, TS, 1, 2, H, DH), (1, TS, 1, 2, H, DH), (1, TS, 2, CW)]


def kernel(**inputs):
    import concourse.bacc as bacc
    from concourse.bass_utils import run_bass_kernel_spmd

    nc = bacc.Bacc("TRN2", target_bir_lowering=False, num_devices=1)
    arrays, args = {}, []
    for name in _INS:
        a = np.ascontiguousarray(inputs[name])
        arrays[f"in_{name}"] = a
        args.append(nc.dram_tensor(f"in_{name}", a.shape, mybir.dt.from_np(a.dtype), kind="ExternalInput").ap())
    for i, shape in enumerate(_OUTS):
        args.append(nc.dram_tensor(f"out_{i}", shape, F32, kind="ExternalOutput").ap())
    hybrid_step(nc, *args)
    r = run_bass_kernel_spmd(nc, [arrays], core_ids=[0])
    return tuple(r.results[0][f"out_{i}"] for i in range(len(_OUTS)))
```

```python
from contextlib import ExitStack

import numpy as np

import concourse.bass as bass
from concourse import mybir

F32 = mybir.dt.float32
F32R = mybir.dt.float32r
I32 = mybir.dt.int32
U32 = mybir.dt.uint32
ALU = mybir.AluOpType
ACT = mybir.ActivationFunctionType
AX = mybir.AxisListType

P = 128
D = 1024
KD = D // P
TP = 512
TS = 8
T = TP + TS
NB = TP // P
HALF = T // 2
G, H, DH = 3, 4, 64
AW = G * H * DH
OW = H * DH
CW = D // 2
CF = CW // P
DIL = (1, 4, 16)
WIN = (128, 512, 2048)
PAST = 1024
SLOPE = (2.0 ** (-8.0 * np.arange(1, G * H + 1) / (G * H))).reshape(G, H)
NG, EG = 4, 8
NE = NG * EG
FF = D // 4
FE = FF // P
EPS = 1e-6
SCALE = DH ** -0.5
BIG = 1e30
SKIP = 1.0e6
R = 64
RBITS = R.bit_length() - 1
OVER = 2 * T // (R + 1)
NTILE = NE + OVER
KEYS = tuple(min(w // d, (PAST if w > PAST else w) // d) for w, d in zip(WIN, DIL))

Q0, K0, V0, B0, C0, U0 = 0, AW // P, 2 * AW // P, 3 * AW // P, (3 * AW + CW) // P, (3 * AW + 2 * CW) // P
GA0 = (3 * AW + 3 * CW) // P
GB0 = GA0 + KD
AT = AW // P
ORDER = ([("v", V0 + f, f) for f in range(AT)] + [("k", K0 + f, f) for f in range(AT)]
         + [("q", Q0 + f, f) for f in range(AT)]
         + [x for f in range(CF) for x in (("c", C0 + f, f), ("u", U0 + f, f))]
         + [("b", B0 + f, f) for f in range(CF)]
         + [x for f in range(KD) for x in (("ga", GA0 + f, f), ("gb", GB0 + f, f))])
NQKV = 3 * AT
NCONV = NQKV + 3 * CF
NEARLY = NCONV + 4
TURNED = (2, 4, 5, 1, 7)
WRING = 2
UNITS = [(b, h) for b in range(NB) for h in range(H)]
ERING = 5
EUN = 4
AHEAD = EUN - 1


def segments(b):
    out = []
    for g in range(G):
        lo = max(0, b - 1) * P if g == 0 else 0
        out.append((lo, (b + 1) * P - lo))
    return out


def hybrid_step(nc, x_prompt, x_sample, kv0, kv1, kv2, cache_conv, c_prompt, c_sample, g_mix, w_ada, b_ada, w_in,
                conv_w, w_pa, w_pb, w_o, g_ffn, w_rg, b_rg, w_re, b_re, w_gate, w_up, w_down, g_final,
                y_prompt, y_sample, p_kv128, p_kv512, p_kv2048, p_conv, s_kv128, s_kv512, s_kv2048, s_conv):
    ctx = ExitStack()
    with ctx:
        ctx.enter_context(nc.allow_non_contiguous_dma(reason="small vectors"))

        def sem(name):
            return ctx.enter_context(nc.semaphore(name))


        layout, at = {}, 0
        for name, n in (("SPLIT", 4 * D + 2 * KD * T), ("RING", WRING * D), ("UC", CF * (T + 2)), ("YC", CF * T),
                        ("CACHE", 6 * D), ("CT", T), ("VTOK", 5 * AW), ("X", 5 * D), ("M", 8 * D + 512),
                        ("QK", 2 * AT * T), ("SMALL", 3984)):
            layout[name] = at
            at += n
        with nc.sbuf_tensor("w_parts", [P, 2, 2, KD, P], F32R) as w_parts, \
                nc.sbuf_tensor("h_parts", [P, 2, KD, T], F32R) as h_parts:
            pass
        near = layout["X"]
        arena = ctx.enter_context(nc.sbuf_tensor("arena", [P, near], F32))
        arena_b = ctx.enter_context(nc.sbuf_tensor("arena_b", [P, at - near], F32))

        def region(name, off, n, rows=P):
            lo = layout[name] + off
            if lo < near:
                assert lo + n <= near
                return arena[0:rows, lo:lo + n]
            return arena_b[0:rows, lo - near:lo - near + n]

        def cube(ap, n):
            return ap.rearrange("p (a b) -> p a b", a=n)

        x = cube(region("X", 0, 5 * D), 5)
        ktok = cube(region("X", 0, 5 * AW), 5)
        prob = cube(region("X", 0, 2 * 1280), 2)
        probT = cube(region("X", 2560, 2 * 512), 2)
        attnT = cube(region("X", 3584, 2 * T), 2)
        otok = region("X", 3584 + 2 * T, OW)
        bias = cube(region("M", 0, 5 * D), H)
        qb = region("M", 5 * D, 2 * D)
        ada_bias = cube(region("M", 5 * D, 12 * P), 12)
        mods = cube(region("M", 7 * D, 12 * P), 12)
        biasS = region("M", 7 * D, H * G * P, TS).rearrange("p (h g r) -> p h g r", h=H, g=G)
        mod_p = cube(region("M", 0, 4 * D), 4)
        mod_s = cube(region("M", 4 * D, 4 * D, TS), 4)
        gffn_b = region("UC", 0, D)
        ring = region("RING", 0, WRING * D).rearrange("p (s k n) -> p s k n", s=WRING, k=KD)
        uT = cube(region("UC", 0, CF * (T + 2)), CF)
        yT = cube(region("YC", 0, CF * T), CF)
        cgate = region("CT", 0, T)
        ustate = region("CT", 0, CW, 2 + TS)
        modT = cube(region("CT", 0, 4 * P), 4)
        g8 = region("CT", 0, P, KD)
        ccrow = region("YC", 0, CW, 19)
        cache = cube(region("CACHE", 0, 6 * D), G)
        wpa = cube(region("CACHE", 0, 2 * D), 2)
        wpb = cube(region("CACHE", 2 * D, 4 * D), CF)
        h_tmp = cube(region("VTOK", D, 3 * TP), 3)
        hs_tmp = cube(region("VTOK", D + 3 * TP, KD * TS), KD)
        vtok = cube(region("VTOK", 0, 5 * AW), 5)
        vst = cube(region("X", 5 * AW, 2 * T), 2)
        crow = region("QK", 4 * D, D, 1 + TS)
        wo0_at = layout["VTOK"] + 5 * AW - 4 * D
        wo = [cube(arena[:, wo0_at:wo0_at + 4 * D], KD), cube(region("SPLIT", 0, 4 * D), KD)]
        ada0 = [region("CACHE", 0, 4 * D), region("SPLIT", 4 * D, 4 * D), region("SPLIT", 8 * D, 4 * D),
                region("QK", 0, 4 * D)]
        ada0 = [cube(r, 2) for r in ada0]
        ada = ada0[0]
        qT = cube(region("QK", 0, AT * T), AT)
        kT = cube(region("QK", AT * T, AT * T), AT)
        mergedT = cube(region("QK", 0, KD * T), KD)
        sig = cube(region("QK", KD * T, 4 * T), 4)
        h2t = cube(region("QK", KD * T, 2 * D), 2)
        delta_i = region("UC", 0, 512).bitcast(I32)
        low2 = region("UC", 512, 512).bitcast(I32)
        low4 = region("UC", 1024, 512).bitcast(I32)
        delta_f = region("UC", 1536, 512)
        nb1 = region("YC", 512, 512)
        nb2 = region("YC", 1024, 512)
        nb0 = region("YC", 1536, 256)
        EW = 6 * D
        gu_at = [region("SPLIT", 4 * D + i * EW, 4 * D) for i in range(3)] + [arena[:, wo0_at:wo0_at + 4 * D]]
        dn_at = [region("SPLIT", 8 * D + i * EW, 2 * D) for i in range(3)] + [region("SPLIT", 0, 2 * D)]
        w_gu = [a.rearrange("p (k a f) -> p k a f", k=KD, a=2) for a in gu_at]
        w_dn = [cube(a, FE) for a in dn_at]
        h2T = cube(region("SPLIT", 4 * D + 3 * EW, D), KD)
        hg = cube(region("SPLIT", 2 * D, 2 * D), EUN)
        qk_work = 2 * AT * T - 2928
        ys = cube(region("QK", qk_work, D), 2)
        hTe = cube(region("QK", qk_work + D, D), 2)
        silu = cube(region("QK", qk_work + 2 * D, 2 * P), 2)
        actv = cube(region("QK", qk_work + 2 * D + 2 * P, 2 * P), 2)
        actT = cube(region("QK", qk_work + 2 * D + 4 * P, 2 * P), 2)
        yk = region("SPLIT", 0, 8 * D).rearrange("p (t k d) -> p t k d", t=4, k=2)
        yk_s = region("SPLIT", 8 * D, 2 * D, TS).rearrange("p (k d) -> p k d", k=2)
        gfin_b = region("SPLIT", 10 * D, D)
        mix = cube(region("SPLIT", 11 * D, 2 * D), 2)
        res = cube(region("SPLIT", 13 * D, 2 * D), 2)

        small = [0]

        def take(n, rows=P):
            small[0] += n
            assert small[0] <= 3984, small[0]
            return region("SMALL", small[0] - n, n, rows)

        ident = take(P)
        cvec = cube(take(KD * 32), KD)
        ccT = cube(take(CF * 19), CF)
        gmixT = take(KD)
        qs = take(AW, TS)
        ks = take(AW, TS)
        selfs = qs[:, 0:OW]
        scS = cube(take(H * 324, TS), H)
        smT = cube(take(G * H * TS), G * H)
        ssq = take(8)
        rstd = take(8)
        minus_half = take(1)
        mx = take(8)
        negm = take(2)
        den = take(2)
        rden = take(2)
        m4 = take(16, TS)
        sc = cube(take(G * H * TS), G)
        wrt = cube(take(KD * 36), KD)
        wk = cube(take(2 * 5), 2)
        rt = [0]

        def rtake(n, rows=P):
            rt[0] += n
            assert rt[0] <= 7 * D
            lo = rt[0] - n
            if lo < 3 * D < rt[0]:
                lo, rt[0] = 4 * D, 4 * D + n
            return region("M", lo, n, rows)

        lgt = cube(rtake(5 * 36), 5)
        rbias = rtake(36)
        iota_e = rtake(NTILE)
        valid = rtake(5)
        tok1 = rtake(5)
        jcol = rtake(1)
        slot_i = rtake(P)
        gmax = rtake(5)
        geq = cube(rtake(5 * 8), 5)
        gidx = rtake(5)
        goh = cube(rtake(5 * 4), 5)
        gexp = cube(rtake(5 * 4), 5)
        ptop = rtake(5)
        prod = rtake(5 * NE).rearrange("p (t g e) -> p t g e", t=5, g=NG)
        sel = cube(rtake(5 * EG), 5)
        vk = cube(rtake(10), 2)
        ik = cube(rtake(10), 2)
        ek = cube(rtake(10), 2)
        ohe = rtake(2 * 5 * NE).rearrange("p (k t e) -> p k t e", k=2, t=5)
        member = cube(rtake(5 * NE), 5)
        past = cube(rtake(6 * NE), 6)
        upper = rtake(P)
        ones = rtake(P)
        ranks = cube(rtake(5 * NE), 5)
        count = rtake(NE)
        extra = rtake(NE)
        extra_i = rtake(NE).bitcast(I32)
        rank_i = cube(rtake(10).bitcast(I32), 2)
        upto = rtake(NE)
        before = rtake(NE)
        tmp2 = rtake(2 * 5 * NE).rearrange("p (k t e) -> p k t e", k=2, t=5)
        rk = cube(rtake(10), 2)
        bk = cube(rtake(10), 2)
        slotk = cube(rtake(10), 2)
        qk_ = cube(rtake(10), 2)
        tilek = cube(rtake(10), 2)
        code = cube(rtake(10), 2)
        t10 = cube(rtake(10), 2)
        oh_slot = rtake(10 * P).rearrange("p (k t s) -> p k t s", k=2, t=5)
        oh_tile = rtake(10 * NTILE).rearrange("p (k t s) -> p k t s", k=2, t=5)
        oh_val = rtake(10 * 2 * NTILE).rearrange("p (k t s) -> p k t s", k=2, t=5)
        lists_f = rtake(2 * NTILE)
        empty = rtake(2 * NTILE)
        lists = cube(rtake(2 * NTILE).bitcast(I32), 2)
        owner_c = region("M", 8 * D, OVER * NE).rearrange("p (o e) -> p o e", o=OVER)
        owner_f = rtake(OVER)
        owner = rtake(OVER).bitcast(I32)
        nover = rtake(1).bitcast(I32)
        gi = rtake(EUN).bitcast(I32)
        si = rtake(EUN).bitcast(I32)

        ps = [ctx.enter_context(nc.psum_tensor(f"bank{i}", [P, 512], F32)) for i in range(8)]

        q_d = nc.dram_tensor("q_scratch", [TS, AW], F32).ap()
        mod_d = nc.dram_tensor("mod_scratch", [1 + TS, 6 * D], F32).ap()
        h_d = nc.dram_tensor("h_scratch", [2 * T, D // 2], F32).ap()
        y_d = nc.dram_tensor("y_scratch", [4 * T, D // 2], F32).ap()

        s_x = [sem(f"s_xin{i}") for i in range(5)]
        s_c = sem("s_c")
        s_ada = [sem(f"s_ada{i}") for i in range(4)]
        s_win = [sem(f"s_win{i}") for i in range(WRING)]
        s_key = sem("s_key")
        s_val = sem("s_val")
        s_wp = sem("s_wp")
        s_wo = sem("s_wo")
        s_xr = [sem(f"s_xr{i}") for i in range(5)]
        s_eg = [sem(f"s_eg{i}") for i in range(EUN)]
        s_ed = [sem(f"s_ed{i}") for i in range(EUN)]
        s_ident = sem("s_ident")
        s_csilu = sem("s_csilu")
        s_cT = sem("s_cT")
        s_cvec = sem("s_cvec")
        s_adamm = sem("s_adamm")
        s_adaev = sem("s_adaev")
        s_modT = sem("s_modT")
        s_modc = sem("s_modc")
        s_mod = sem("s_mod")
        s_sq = sem("s_sq")
        s_ms = sem("s_ms")
        s_rstd = sem("s_rstd")
        s_xn = sem("s_xn")
        s_xT = sem("s_xT")
        s_hA = sem("s_hA")
        s_hD = sem("s_hD")
        s_whi = sem("s_whi")
        s_wlo = sem("s_wlo")
        s_gfu = sem("s_gfu")
        s_half = sem("s_half")
        s_wr = sem("s_wr")
        s_feat = sem("s_feat")
        s_tokT = sem("s_tokT")
        s_tok = sem("s_tok")
        s_bias = sem("s_bias")
        s_kv = sem("s_kv")
        s_modw = sem("s_modw")
        s_modr = sem("s_modr")
        s_qw = sem("s_qw")
        s_qr = sem("s_qr")
        s_kq = sem("s_kq")
        s_kqp = sem("s_kqp")
        s_qk = sem("s_qk")
        s_sread = sem("s_sread")
        s_neg = sem("s_neg")
        s_exp = sem("s_exp")
        s_pT = sem("s_pT")
        s_even = sem("s_even")
        s_odd = sem("s_odd")
        s_pv = sem("s_pv")
        s_o = sem("s_o")
        s_smp = sem("s_smp")
        s_self = sem("s_self")
        s_smpv = sem("s_smpv")
        s_smo = sem("s_smo")
        s_u = sem("s_u")
        s_cg = sem("s_cg")
        s_yb = sem("s_yb")
        s_ustw = sem("s_ustw")
        s_sig = sem("s_sig")
        s_proj = sem("s_proj")
        s_mrg = sem("s_mrg")
        s_a2 = sem("s_a2")
        s_wom = sem("s_wom")
        s_x2 = sem("s_x2")
        s_sq2 = sem("s_sq2")
        s_h2 = sem("s_h2")
        s_h2w = [sem(f"s_h2w{i}") for i in range(2)]
        s_h2T = sem("s_h2T")
        s_h2c = sem("s_h2c")
        s_rt = sem("s_rt")
        s_rw = sem("s_rw")
        s_rp = sem("s_rp")
        s_ra = sem("s_ra")
        s_rc = sem("s_rc")
        s_lists = sem("s_lists")
        s_hz = sem("s_hz")
        s_hg = [sem(f"s_hg{i}") for i in range(EUN)]
        s_gx = sem("s_gx")
        s_sx = sem("s_sx")
        s_t = sem("s_t")
        s_te = sem("s_te")
        s_gu = sem("s_gu")
        s_si = sem("s_si")
        s_am = sem("s_am")
        s_ta = sem("s_ta")
        s_at = sem("s_at")
        s_y = sem("s_y")
        s_ye = sem("s_ye")
        s_sc = [sem(f"s_sc{i}") for i in range(2)]
        s_go = sem("s_go")
        s_moe = sem("s_moe")
        s_yk = [sem(f"s_yk{i}") for i in range(5)]
        s_gf = sem("s_gf")
        s_w0 = sem("s_w0")
        s_mix = sem("s_mix")
        s_mixg = sem("s_mixg")
        s_sq3 = sem("s_sq3")
        s_x3 = sem("s_x3")
        s_res = sem("s_res")
        s_out = [sem(f"s_out{i}") for i in range(2)]
        s_dve = sem("s_dve")
        s_pool = sem("s_pool")
        s_act = sem("s_act")

        plan, batches = [], []
        halves = [(n, s) for n in range(NQKV, NEARLY) for s in range(2)]
        hc = [0]

        def more_halves(k, last=NCONV):
            while k and hc[0] < len(halves) and halves[hc[0]][0] < last:
                plan.append(("half", *halves[hc[0]]))
                hc[0] += 1
                k -= 1

        def unit_batches(u):
            b = UNITS[u][0]
            chunks = [(g, lo // P + c) for g, (lo, n) in enumerate(segments(b)) for c in range(n // P)]
            got = []
            for a in range(0, len(chunks), 4):
                got.append(len(batches))
                batches.append(("p", u, a, chunks[a:a + 4], a == 0, a + 4 >= len(chunks)))
            return got

        def turn(u, fill, last, then=None):
            got = unit_batches(u)
            plan.append(("turn", got[0]))
            for a, i in enumerate(got):
                if a + 1 < len(got):
                    plan.append(("turn", got[a + 1]))
                if a + 1 == len(got) or a == 0 and len(got) > 2:
                    more_halves(min(fill, 1), last)
                    fill -= 1
                if a == len(got) - 1:
                    plan.extend(then or [])
                plan.append(("pv", i))

        NU = len(UNITS)
        S_AT = 12

        def no(u):
            return u + (u >= S_AT)

        for s in range(NU + 1):
            late = NEARLY if s >= NU - 1 else NCONV
            if s == S_AT:
                plan.append(("qs",))
            if s < NU:
                plan.append(("qk", s))
            more_halves(1, late)
            if s in (3, 6, 9):
                plan.append(("samples", s // 3 - 1))
            if s >= 1:
                if (s - 1) % H == 0 and s > 1:
                    plan.append(("turn_o", len(batches), (s - 1) // H - 1))
                    batches.append(("o", (s - 1) // H - 1))
                turn(s - 1, 2 if s >= NU - 1 else s % 2, late, [("exp", s)] if s < NU else None)
            else:
                plan.append(("exp", s))
            if s == S_AT + 1:
                plan.append(("turn_s", len(batches)))
                batches.append(("s",))
                plan.append(("pv_s",))
        more_halves(2, NEARLY)
        plan.append(("turn_o", len(batches), NB - 1))
        batches.append(("o", NB - 1))
        more_halves(99, NEARLY)
        plan.append(("turn_u", len(batches)))
        batches.append(("u",))
        pv_after, n_pv = {}, 0
        for i, bt in enumerate(batches):
            n_pv += bt[0] == "p"
            pv_after[i] = n_pv
        NPV = n_pv
        unit_end = {bt[1]: pv_after[i] for i, bt in enumerate(batches) if bt[0] == "p" and bt[5]}

        def width(b):
            return sum(n for _, n in segments(b))

        RB = [(4 if i == 0 else i - 1) for i in range(5)]
        rows = [P, P, P, P, TS]

        kv = (kv0, kv1, kv2)
        p_kv = (p_kv128, p_kv512, p_kv2048)
        s_kvo = (s_kv128, s_kv512, s_kv2048)
        win_v = w_in[0].rearrange("(k p) (t n) -> t p k n", p=P, n=P)
        ada_v = w_ada[0].rearrange("(s k p) (g n) -> g s k p n", k=2, p=P, g=3)
        xp_v = x_prompt[0].rearrange("(t p) d -> t p d", p=P)
        yp_v = y_prompt[0].rearrange("(t p) d -> t p d", p=P)
        xs_v = x_sample.rearrange("b o d -> (b o) d")
        ys_v = y_sample.rearrange("b o d -> (b o) d")
        wo_v = w_o[0].rearrange("(k p) n -> p k n", p=P)
        wg_v = w_gate[0].rearrange("e (j p c) f -> e p j c f", j=2, p=P)
        wu_v = w_up[0].rearrange("e (j p c) f -> e p j c f", j=2, p=P)
        wd_v = w_down[0].rearrange("e (c p) d -> e p c d", p=P)

        def at_least(eng, s, v):
            if not (isinstance(v, int) and v <= 0):
                eng.wait_ge(s, v)

        block = ctx.enter_context(nc.Block())

        @block.sync
        def _(sp):
            sp.dma_start(crow[0:1], c_prompt).then_inc(s_c, 16)
            sp.dma_start(crow[1:1 + TS], c_sample).then_inc(s_c, 16)
            sp.dma_start(ccrow[0:2 * TS], cache_conv[0].rearrange("b j c -> (b j) c")).then_inc(s_c, 16)
            sp.dma_start(ccrow[2 * TS:2 * TS + 3], conv_w[0]).then_inc(s_c, 16)
            sp.dma_start(g8, g_mix.rearrange("o (k p) -> (o k) p", p=P)).then_inc(s_c, 16)
            for j in range(4):
                src = b_ada[0].rearrange("(g j s n) -> j g (s n)", g=3, j=4, s=4)[j:j + 1]
                sp.dma_start(ada_bias[32 * j:32 * j + 32].rearrange("p (g s) n -> p g (s n)", g=3),
                             src.to_broadcast([32, 3, 512])).then_inc(s_c, 16)

            def load_ada(a):
                if a >= 4:
                    sp.wait_ge(s_adamm, a)
                dst = ada0[a] if a < 4 else ada
                for k in range(2):
                    sp.dma_start(dst[:, k], ada_v[a // 4, a % 4, k]).then_inc(s_ada[min(a, 3)], 16)

            for a in range(4):
                load_ada(a)
                if a == 1:
                    for i in range(5):
                        sp.dma_start(x[0:rows[i], i], xp_v[i] if i < 4 else xs_v).then_inc(s_x[i], 16)
            for n in range(len(ORDER)):
                if n == NQKV + 2:
                    sp.wait_ge(s_adamm, 12)
                    for g in range(G):
                        src = kv[g][0].rearrange("b (r s) a h d -> s r a b (h d)", s=DIL[g])[0, :, 0]
                        sp.dma_start(cache[0:KEYS[g], g].rearrange("p (b f) -> p b f", b=TS), src).then_inc(s_key, 16)
                if n >= WRING:
                    sp.wait_ge(s_wlo, n - WRING + 1)
                sp.dma_start(ring[:, n % WRING], win_v[ORDER[n][1]]).then_inc(s_win[n % WRING], 16)
                if n % 2 == 1 and 4 <= (n + 5) // 2 < 12:
                    load_ada((n + 5) // 2)
                if n == NCONV + 1:
                    sp.wait_ge(s_smpv, 1)
                    sp.dma_start(wpa, w_pa[0].rearrange("(c p) n -> p c n", p=P)).then_inc(s_wp, 16)
                    sp.dma_start(wpb, w_pb[0].rearrange("(c p) n -> p c n", p=P)).then_inc(s_wp, 16)
                if n == NCONV + 6:
                    sp.wait_ge(s_pv, NPV)
                    sp.wait_ge(s_ustw, 32)
                    sp.dma_start(wo[0], wo_v[:, :, 0:512]).then_inc(s_wo, 16)
            sp.wait_ge(s_half, 2 * len(ORDER))
            sp.dma_start(wo[1], wo_v[:, :, 512:1024]).then_inc(s_wo, 16)
            sp.dma_start(wrt[:, :, 0:NG], w_rg[0].rearrange("(k p) n -> p k n", p=P)).then_inc(s_wr, 16)
            sp.dma_start(wrt[:, :, NG:NG + NE], w_re[0].rearrange("(k p) n -> p k n", p=P)).then_inc(s_wr, 16)
            sp.wait_ge(s_proj, KD)
            for i in RB:
                sp.dma_start(x[0:rows[i], i], xp_v[i] if i < 4 else xs_v).then_inc(s_xr[i], 16)
            sp.wait_ge(s_mrg, KD)
            sp.wait_ge(s_gfu, 1)

            def load_gate_up(e, j):
                wgu = w_gu[j].rearrange("p (j c) a f -> p j c a f", j=2)
                for src, a in ((wg_v, 0), (wu_v, 1)):
                    s1 = src[e] if isinstance(e, int) else src[bass.ds(e, 1)].rearrange("o p j c f -> (o p) j c f")
                    for jj in range(2):
                        sp.dma_start(wgu[:, jj, :, a], s1[:, jj]).then_inc(s_eg[j], 16)

            def load_down(e, j):
                s1 = wd_v[e] if isinstance(e, int) else wd_v[bass.ds(e, 1)].rearrange("o p c d -> (o p) c d")
                sp.dma_start(w_dn[j], s1).then_inc(s_ed[j], 16)

            for j in range(EUN):
                if j == EUN - 1:
                    sp.wait_ge(s_wom, 10)
                load_gate_up(j, j)
                load_down(j, j)
            with sp.Fori(1, NE // EUN) as it:
                for j in range(EUN):
                    sp.wait_ge(s_gu, EUN * it + (j + 1 - EUN))
                    load_gate_up(EUN * it + j, j)
                    sp.wait_ge(s_y, EUN * it + (j + 1 - EUN))
                    load_down(EUN * it + j, j)
            sp.wait_ge(s_lists, 1)
            n_over = sp.value_load(nover[0:1, 0:1], min_val=0, max_val=OVER)
            with sp.If(n_over > 0):
                with sp.Fori(0, n_over) as o:
                    sp.wait_ge(s_y, o + NE)
                    e = sp.value_load(owner[0:1, bass.ds(o, 1)], min_val=0, max_val=NE - 1)
                    load_gate_up(e, 0)
                    load_down(e, 0)
            sp.wait_ge(s_moe, 1)
            y4 = y_d.rearrange("(t k j) d -> t k (j d)", k=2, j=2)
            for i in RB:
                if i < 4:
                    sp.dma_start(yk[:, i], y4[i * P:(i + 1) * P]).then_inc(s_yk[i], 16)
                else:
                    sp.dma_start(yk_s, y4[TP:T]).then_inc(s_yk[i], 16)
                if i == 0:
                    sp.dma_start(gfin_b, g_final.rearrange("(o d) -> o d", o=1).to_broadcast([P, D])).then_inc(s_gf, 16)
            for n, i in enumerate(RB):
                sp.wait_ge(s_res, n + 1)
                sp.dma_start(yp_v[i] if i < 4 else ys_v, res[0:rows[i], n % 2]).then_inc(s_out[n % 2], 16)
            sp.wait_ge(s_out[0], 16 * 3)
            sp.wait_ge(s_out[1], 16 * 2)

        @block.gpsimd
        def _(pool):
            own = [0]

            def inverse_root(n, i):
                pool.wait_ge(s_ms, n + 1)
                t = rstd[0:rows[i], i:i + 1]
                pool.tensor_tensor(t, t, minus_half[0:rows[i]], ALU.pow).then_inc(s_rstd, 1)

            def link(ins):
                own[0] += 1
                ins.then_inc(s_pool, 1)
                pool.wait_ge(s_pool, own[0])

            pool.memset(minus_half, -0.5)
            link(pool.memset(ident, 1.0))
            link(pool.affine_select(out=ident, in_=ident, compare_op=ALU.is_equal, fill=0.0, base=0,
                                    pattern=[[-1, P]], channel_multiplier=1))
            pool.engine_nop().then_inc(s_ident, 1)
            pool.iota(delta_i, pattern=[[-1, 512]], base=384, channel_multiplier=1).then_inc(s_bias, 1)
            pool.iota(delta_f, pattern=[[-1, 512]], base=384, channel_multiplier=1,
                      allow_small_or_imprecise_dtypes=True).then_inc(s_bias, 1)
            link(pool.iota(nb0, pattern=[[1, 256]], base=-P, channel_multiplier=-1,
                           allow_small_or_imprecise_dtypes=True))
            link(pool.affine_select(out=nb0, in_=nb0, compare_op=ALU.is_ge, fill=-BIG, base=P,
                                    pattern=[[-1, 256]], channel_multiplier=1))
            link(pool.affine_select(out=nb0, in_=nb0, compare_op=ALU.is_ge, fill=-BIG, base=0,
                                    pattern=[[1, 256]], channel_multiplier=-1))
            for i in range(5):
                inverse_root(i, i)
            pool.wait_ge(s_bias, 4)
            for nb in (nb1, nb2):
                link(pool.affine_select(out=nb, in_=nb, compare_op=ALU.is_ge, fill=-BIG, base=384,
                                        pattern=[[-1, 512]], channel_multiplier=1))
            for h in range(H):
                for g, nb, lo, n in ((0, nb0, 0, 256), (1, nb1, 256, 512), (2, nb2, 768, 512)):
                    ins = pool.tensor_scalar(bias[:, h, lo:lo + n], nb, float(SLOPE[g, h] / SCALE), None, ALU.mult)
            link(ins)
            for f in range(CF):
                link(pool.memset(uT[:, f, 0:2], 0.0))
            pool.engine_nop().then_inc(s_bias, 1)
            pool.wait_ge(s_tok, 2 * AT)
            n_kv = 0
            for g in range(G):
                nt = p_kv[g].shape[2] // P
                for a, (tok, stok) in enumerate(((ktok, ks), (vtok, vtok[0:TS, 4]))):
                    dst = p_kv[g][0, 0].rearrange("(t p) a h d -> p t a (h d)", p=P)[:, :, a]
                    pool.dma_start(dst, tok[:, 4 - nt:4, g * OW:(g + 1) * OW]).then_inc(s_kv, 16)
                    pool.dma_start(s_kvo[g][0, :, 0].rearrange("b a h d -> b a (h d)")[:, a],
                                   stok[:, g * OW:(g + 1) * OW]).then_inc(s_kv, 16)
                    n_kv += 2
            pool.dma_start(s_conv[0, :, 0], cache_conv[0, :, 1]).then_inc(s_kv, 16)
            pool.wait_ge(s_kv, 16 * (n_kv + 1))
            pool.engine_nop().then_inc(s_bias, 1)
            pool.wait_ge(s_adaev, 3)
            for j in range(4):
                dst = mod_d.rearrange("r (g j n) -> j r g n", g=3, j=4)[j][:, 1:3]
                pool.dma_start(dst, mods[32 * j:32 * j + 1 + TS, 4:12].rearrange("p (g s) n -> p g (s n)", g=2)
                               ).then_inc(s_modw, 16)
            pool.wait_ge(s_tok, NQKV)
            pool.dma_start(q_d, qs).then_inc(s_qw, 16)
            pool.wait_ge(s_qw, 16)
            pool.wait_ge(s_modw, 64)
            for g in range(G):
                if g:
                    pool.wait_ge(s_kqp, g)
                pool.dma_start(qb.rearrange("p (b f) -> p b f", b=TS),
                               q_d[:, g * OW:(g + 1) * OW].rearrange("(o b) f -> o b f", o=1)
                               .to_broadcast([P, TS, OW])).then_inc(s_qr, 16)
            for h in range(H):
                for g in range(G):
                    pool.iota(biasS[:, h, g], pattern=[[DIL[g], P]], base=-DIL[g] * KEYS[g], channel_multiplier=0,
                              allow_small_or_imprecise_dtypes=True)
            link(pool.engine_nop())
            for h in range(H):
                for g in range(G):
                    ins = pool.tensor_scalar(biasS[:, h, g], biasS[:, h, g], float(SLOPE[g, h] / SCALE), None, ALU.mult)
            link(ins)
            pool.engine_nop().then_inc(s_bias, 1)
            pool.wait_ge(s_kq, G)
            for g in range(G):
                src = kv[g][0].rearrange("b (r s) a h d -> s r a b (h d)", s=DIL[g])[0, :, 1]
                pool.dma_start(cache[0:KEYS[g], g].rearrange("p (b f) -> p b f", b=TS), src).then_inc(s_val, 16)
            pool.wait_ge(s_sread, G * (NU + 1))
            md = mod_d[:, 2 * D:6 * D].rearrange("r (v d) -> r v d", v=4)
            pool.dma_start(mod_p, md[0:1].to_broadcast([P, 4, D])).then_inc(s_modr, 16)
            pool.dma_start(mod_s, md[1:1 + TS]).then_inc(s_modr, 16)
            pool.wait_ge(s_odd if (len(batches) - 1) % 2 else s_even, (len(batches) - 1) // 2 + 1)
            pool.dma_start(gffn_b, g_ffn.to_broadcast([P, D])).then_inc(s_modr, 16)
            pool.dma_start(p_conv[0, 0], ustate[0:2]).then_inc(s_ustw, 16)
            pool.dma_start(s_conv[0, :, 1], ustate[2:2 + TS]).then_inc(s_ustw, 16)
            pool.wait_ge(s_ustw, 32)
            for n, i in enumerate(RB):
                inverse_root(5 + n, i)
                pool.wait_ge(s_h2, n + 1)
                dst = h_d.rearrange("(t j) d -> t (j d)", j=2)[i * P:i * P + rows[i]]
                pool.dma_start(dst, h2t[0:rows[i], n % 2]).then_inc(s_h2w[n % 2], 16)
            pool.wait_ge(s_h2, 5)
            f = dict(allow_small_or_imprecise_dtypes=True)
            pool.iota(iota_e, pattern=[[1, NTILE]], base=0, channel_multiplier=0, **f)
            pool.iota(slot_i.rearrange("p (j s) -> p j s", j=2), pattern=[[0, 2], [1, R]], base=0,
                      channel_multiplier=0, **f)
            pool.iota(tok1, pattern=[[P, 5]], base=1, channel_multiplier=1, **f)
            pool.memset(valid, 1.0)
            pool.memset(jcol, 0.0)
            pool.memset(upper, 1.0)
            link(pool.memset(ones, 1.0))
            link(pool.affine_select(out=valid[:, 4:5], in_=valid[:, 4:5], compare_op=ALU.is_ge, fill=0.0, base=TS - 1,
                                    pattern=[[0, 1]], channel_multiplier=-1))
            link(pool.affine_select(out=jcol, in_=jcol, compare_op=ALU.is_ge, fill=1.0, base=R - 1,
                                    pattern=[[0, 1]], channel_multiplier=-1))
            link(pool.affine_select(out=upper, in_=upper, compare_op=ALU.is_gt, fill=0.0, base=0,
                                    pattern=[[1, P]], channel_multiplier=-1))
            link(pool.tensor_tensor(tok1, tok1, valid, ALU.mult))
            pool.dma_start(rbias[:, 0:NG], b_rg.to_broadcast([P, NG])).then_inc(s_rc, 16)
            pool.dma_start(rbias[:, NG:NG + NE], b_re.to_broadcast([P, NE])).then_inc(s_rc, 16)
            pool.wait_ge(s_h2c, 10)
            pool.wait_ge(s_rt, 5)
            link(pool.memset(hg.rearrange("p a b -> p (a b)"), 0.0))
            pool.wait_ge(s_lists, 1)
            pool.wait_ge(s_h2w[0], 48)
            pool.wait_ge(s_h2w[1], 32)
            last_read, last_written = pool.to_reg(2 * T - 1), pool.to_reg(4 * T - 1)

            def apart(s, v):
                if not (isinstance(v, int) and v <= 0):
                    pool.wait_ge(s, v)
                    pool.sem_inc(s_go, 1)

            def gather(e, j, ix):
                apart(s_t, e - EUN + 1)
                pool.tensor_copy(gi[:, j:j + 1], lists[:, 1, ix]).then_inc(s_gx, 1)
                apart(s_gx, e + 1)
                pool.indirect_dma_start(out=hg[:, j], out_offset=None, in_=h_d,
                                        in_offset=bass.IndirectOffsetOnAxis(ap=gi[:, j:j + 1], axis=0),
                                        bounds_check=last_read, oob_is_err=False).then_inc(s_hg[j], 16)

            def scatter(e, j, ix):
                pool.tensor_copy(si[:, j:j + 1], lists[:, 0, ix]).then_inc(s_sx, 1)
                apart(s_sx, e + 1)
                apart(s_ye, e + 1)
                b = j % 2
                pool.indirect_dma_start(out=y_d, out_offset=bass.IndirectOffsetOnAxis(ap=si[:, j:j + 1], axis=0),
                                        in_=ys[:, b], in_offset=None,
                                        bounds_check=last_written, oob_is_err=False).then_inc(s_sc[b], 16)

            def column(e):
                return slice(e, e + 1) if isinstance(e, int) else bass.ds(e, 1)

            def four(it, last=False):
                e0 = EUN * it
                for j in range(EUN):
                    ahead = j + AHEAD
                    if not last or ahead < EUN:
                        gather(e0 + ahead, ahead % EUN, column(e0 + ahead))
                    scatter(e0 + j, j, column(e0 + j))

            for e in range(AHEAD):
                gather(e, e, column(e))
            four(0)
            with pool.Fori(1, NE // EUN - 1) as it:
                four(it)
            four(NE // EUN - 1, True)
            n_over = pool.value_load(nover[0:1, 0:1], min_val=0, max_val=OVER)
            with pool.If(n_over > 0):
                with pool.Fori(0, n_over) as o:
                    apart(s_ye, o + NE)
                    gather(o + NE, 0, bass.ds(o + NE, 1))
                    scatter(o + NE, 0, bass.ds(o + NE, 1))
                    apart(s_sc[0], 16 * o + (16 * (NE // 2) + 16))
            pool.wait_ge(s_sc[0], 16 * (NE // 2))
            pool.wait_ge(s_sc[1], 16 * (NE // 2))
            pool.engine_nop().then_inc(s_moe, 1)
            for n, i in enumerate(RB):
                r = rows[i]
                md = mod_p if i < 4 else mod_s
                pool.wait_ge(s_mix, n + 1)
                pool.tensor_tensor(mix[0:r, n % 2], mix[0:r, n % 2], md[0:r, 3], ALU.mult).then_inc(s_mixg, 1)
                if n:
                    inverse_root(10 + n - 1, RB[n - 1])
            inverse_root(14, RB[4])

        def copy_h2(act, n):
            r = rows[RB[n]]
            for c in range(2):
                act.wait_ge(s_h2T, 2 * n + c + 1)
                if n and c == 0:
                    act.wait_ge(s_rt, n)
                act.activation(h2T[:, 4 * c:4 * c + 4, 0:r],
                               ps[6 + c][:].rearrange("p (k t) -> p k t", k=4)[:, :, 0:r], ACT.Copy).then_inc(s_h2c, 1)

        @block.scalar
        def _(act):
            act.wait_ge(s_c, 16 * 9)
            act.activation(crow, crow, ACT.Silu).then_inc(s_csilu, 1)
            for i in range(5):
                act.wait_ge(s_x[i], 16)
                at_least(act, s_sq, i)
                act.activation(region("VTOK", 0, D, rows[i]),
                               x[0:rows[i], i], ACT.Square, accum_out=ssq[0:rows[i], i:i + 1]).then_inc(s_sq, 1)
            act.wait_ge(s_mod, 1)
            for k in range(KD):
                act.wait_ge(s_xT, k + 2)
                j, cc = k // 4, k % 4
                at_least(act, s_hD, k - 1)
                for dst in (h_tmp[:, k % 3], h_parts[:, 0, k, 0:TP])[0:2 - k % 2]:
                    ins = act.activation(dst, ps[TURNED[k % 5]][:], ACT.Identity,
                                         bias=modT[:, cc, 32 * j:32 * j + 1],
                                         scale=modT[:, cc, 64 + 32 * j:65 + 32 * j])
                ins.then_inc(s_hA, 1)

            def split(n):
                if n < len(ORDER):
                    act.wait_ge(s_win[n % WRING], 16 * (n // WRING + 1))
                    at_least(act, s_half, 2 * (n - 1))
                    act.activation(w_parts[:, n % 2, 0], ring[:, n % WRING], ACT.Copy).then_inc(s_whi, 1)

            def feature(n, s):
                kind, _, f = ORDER[n]
                if s == 0:
                    split(n + 1)
                if kind in "ub":
                    return
                act.wait_ge(s_half, 2 * n + s + 1)
                src = ps[s][:, 0:HALF]
                span = slice(s * HALF, (s + 1) * HALF)
                if kind in "vkq":
                    if kind == "v" and s == 0:
                        at_least(act, s_tokT, n - 1)
                    dst = {"v": vst[:, n % 2], "k": kT[:, f], "q": qT[:, f]}[kind]
                    act.activation(dst[:, span], src, ACT.Copy).then_inc(s_feat, 1)
                elif kind == "c":
                    if f:
                        act.wait_ge(s_u, 2 * f)
                    act.activation(cgate[:, span], src, ACT.Copy).then_inc(s_cg, 1)
                elif kind in ("ga", "gb"):
                    if n == NCONV and s == 0:
                        act.wait_ge(s_qk, G * (NU + 1))
                    if f >= 2 and s == 0:
                        act.wait_ge(s_mrg, f - 1)
                    dst = sig[:, (0 if kind == "ga" else 2) + f % 2]
                    act.activation(dst[:, span], src, ACT.Sigmoid).then_inc(s_sig, 1)

            split(0)
            for n in range(NQKV):
                for s in range(2):
                    feature(n, s)
            act.wait_ge(s_bias, 6)
            for what, *a in plan:
                if what == "half":
                    feature(*a)
                elif what.startswith("turn"):
                    i = a[0]
                    bank = ps[5 + i % 2]
                    act.wait_ge(s_pT, i + 1)
                    if what == "turn":
                        n = len(batches[i][3]) * P
                        at_least(act, s_pv, pv_after[i - 2] if i >= 2 else 0)
                        ins = act.activation(probT[:, i % 2, 0:n], bank[:, 0:n], ACT.Copy)
                    elif what == "turn_o":
                        ins = act.activation(attnT[:, :, a[1] * P:(a[1] + 1) * P],
                                             bank[:, 0:2 * P].rearrange("p (c t) -> p c t", c=2), ACT.Copy)
                    elif what == "turn_s":
                        flat = smT.rearrange("p a b -> p (a b)")
                        act.activation(flat[:, 0:64], bank[:, 0:64], ACT.Copy)
                        ins = act.activation(flat[0:64, 64:96], bank[0:64, 64:96], ACT.Copy)
                    else:
                        ins = act.activation(ustate, bank[0:2 + TS, :], ACT.Copy)
                    ins.then_inc(s_odd if i % 2 else s_even, 1)
                if what == "exp":
                    u = a[0]
                    b = UNITS[u][0]
                    act.wait_ge(s_neg, no(u) + 1)
                    act.activation(prob[:, u % 2, 0:width(b)], prob[:, u % 2, 0:width(b)], ACT.Exp,
                                   bias=negm[:, u % 2:u % 2 + 1], accum_out=den[:, u % 2:u % 2 + 1]
                                   ).then_inc(s_exp, 1)
                elif what == "qs":
                    act.wait_ge(s_neg, S_AT + 1)
                    act.activation(scS[:, :, 0:323], scS[:, :, 0:323], ACT.Exp).then_inc(s_exp, 1)
            for n in range(NEARLY, len(ORDER)):
                for s in range(2):
                    feature(n, s)
            for n, i in enumerate(RB):
                r = rows[i]
                if n:
                    copy_h2(act, n - 1)
                act.wait_ge(s_x2, n + 1)
                act.activation(h2t[0:r, n % 2], x[0:r, i], ACT.Square, accum_out=ssq[0:r, i:i + 1]).then_inc(s_sq2, 1)
            copy_h2(act, 4)
            act.wait_ge(s_rw, 1)
            act.activation(gexp, gexp, ACT.Exp).then_inc(s_ra, 1)
            act.wait_ge(s_rw, 2)
            act.activation(wk[:, 1], wk[:, 1], ACT.Exp).then_inc(s_ra, 1)

            def expert(e, j, last=None):
                b = j % 2
                act.wait_ge(s_t, e + 1)
                at_least(act, s_gu, e - 1)
                act.activation(hTe[:, b], ps[b][:], ACT.Copy).then_inc(s_te, 1)

            def silu_of(e, j):
                b = j % 2
                act.wait_ge(s_gu, e + 1)
                at_least(act, s_am, e - 1)
                act.activation(silu[:, b], ps[2 + b][:, 0:P], ACT.Silu).then_inc(s_si, 1)

            def four(it, last=False):
                e0 = EUN * it
                for j in range(EUN):
                    if not last or j + 1 < EUN:
                        expert(e0 + (j + 1), j + 1)
                    silu_of(e0 + j, j)

            expert(0, 0)
            four(0)
            with act.Fori(1, NE // EUN - 1) as it:
                four(it)
            four(NE // EUN - 1, True)
            act.wait_ge(s_lists, 1)
            n_over = act.value_load(nover[0:1, 0:1], min_val=0, max_val=OVER)
            with act.If(n_over > 0):
                with act.Fori(0, n_over) as o:
                    expert(o + NE, 0)
                    silu_of(o + NE, 0)
            def weigh(n):
                i = RB[n]
                r = rows[i]
                pair = yk[:, i] if i < 4 else yk_s
                act.wait_ge(s_yk[i], 16)
                act.activation(pair[0:r, 0], pair[0:r, 0], ACT.Copy, scale=wk[0:r, 0, i:i + 1]).then_inc(s_w0, 1)

            weigh(0)
            weigh(1)
            for n, i in enumerate(RB):
                r = rows[i]
                if n + 2 < 5:
                    weigh(n + 2)
                act.wait_ge(s_x3, n + 1)
                act.activation(mix[0:r, n % 2], x[0:r, i], ACT.Square, accum_out=ssq[0:r, i:i + 1]).then_inc(s_sq3, 1)

        @block.vector
        def _(dve):
            own = [0]

            def link(ins):
                own[0] += 1
                ins.then_inc(s_dve, 1)
                dve.wait_ge(s_dve, own[0])

            link(dve.memset(cvec.rearrange("p k r -> p (k r)"), 0.0))
            dve.wait_ge(s_bias, 2)
            dve.tensor_scalar(low2, delta_i, DIL[1] - 1, None, ALU.bitwise_and)
            link(dve.tensor_scalar(low4, delta_i, DIL[2] - 1, None, ALU.bitwise_and))
            for nb, low in ((nb1, low2), (nb2, low4)):
                dve.scalar_tensor_tensor(out=nb, in0=low, scalar=-BIG, in1=delta_f, op0=ALU.mult,
                                         op1=ALU.subtract).then_inc(s_bias, 1)
            dve.wait_ge(s_cT, 1)
            dve.tensor_copy(cvec[:, :, 0:1 + TS], cube(ps[2][:, 0:KD * 32], KD)[:, :, 0:1 + TS])
            dve.tensor_copy(ccT, cube(ps[3][:, 0:CF * 32], CF)[:, :, 0:19])
            dve.tensor_copy(gmixT, ps[3][:, CF * 32:CF * 32 + KD]).then_inc(s_cvec, 1)
            for i in range(5):
                r = rows[i]
                dve.wait_ge(s_sq, i + 1)
                dve.tensor_scalar(rstd[0:r, i:i + 1], ssq[0:r, i:i + 1], 1.0 / D, EPS, ALU.mult, ALU.add).then_inc(s_ms, 1)
                dve.wait_ge(s_rstd, i + 1)
                dve.tensor_scalar(x[0:r, i], x[0:r, i], rstd[0:r, i:i + 1], None, ALU.mult).then_inc(s_xn, 1)

            def ada_out(g):
                dve.wait_ge(s_adamm, 4 * g + 4)
                dve.tensor_tensor(mods[:, 4 * g:4 * g + 4], cube(ps[6 + g % 2][:], 4), ada_bias[:, 4 * g:4 * g + 4],
                                  ALU.add).then_inc(s_adaev, 1)

            ada_out(0)
            dve.wait_ge(s_modT, 1)
            link(dve.tensor_copy(modT, cube(ps[0][:], 4)))
            for k in range(KD):
                m = modT[:, k % 4, 64 + 32 * (k // 4):64 + 32 * (k // 4) + 1 + TS]
                ins = dve.tensor_scalar(m, m, 1.0, gmixT[:, k:k + 1], ALU.add, ALU.mult)
            link(ins)
            dve.engine_nop().then_inc(s_mod, 1)
            dve.wait_ge(s_xT, 1)
            for j in range(2):
                link(dve.tensor_tensor(hs_tmp[:, 4 * j:4 * j + 4], cube(ps[3][:, 4 * TS * j:4 * TS * (j + 1)], 4),
                                       modT[:, :, 65 + 32 * j:65 + 32 * j + TS], ALU.mult))
                link(dve.tensor_tensor(hs_tmp[:, 4 * j:4 * j + 4], hs_tmp[:, 4 * j:4 * j + 4],
                                       modT[:, :, 1 + 32 * j:1 + 32 * j + TS], ALU.add))
            link(dve.tensor_copy(h_parts[:, 0, :, TP:T], hs_tmp))
            dve.tensor_tensor(h_parts[:, 1, :, TP:T], hs_tmp, h_parts[:, 0, :, TP:T], ALU.subtract).then_inc(s_hD, 1)
            for k in range(KD):
                dve.wait_ge(s_hA, k + 1)
                if k % 2:
                    link(dve.tensor_copy(h_parts[:, 0, k, 0:TP], h_tmp[:, k % 3]))
                dve.tensor_tensor(h_parts[:, 1, k, 0:TP], h_tmp[:, k % 3], h_parts[:, 0, k, 0:TP], ALU.subtract
                                  ).then_inc(s_hD, 1)

            def split(n):
                if n < len(ORDER):
                    dve.wait_ge(s_whi, n + 1)
                    dve.tensor_tensor(w_parts[:, n % 2, 1], ring[:, n % WRING], w_parts[:, n % 2, 0], ALU.subtract
                                      ).then_inc(s_wlo, 1)

            split(0)

            def by_rows(n):
                kind, _, f = ORDER[n]
                dve.wait_ge(s_tokT, n + 1)
                pr, sm = ps[2 + 2 * (n % 2)], ps[3 + 2 * (n % 2)]
                cols = slice(f * P, (f + 1) * P)
                if kind != "q":
                    tok = vtok if kind == "v" else ktok
                    dve.tensor_copy(tok[:, 0:NB, cols], cube(pr[:], NB))
                dst = {"v": vtok[0:TS, NB, cols], "k": ks[:, cols], "q": qs[:, cols]}[kind]
                dve.tensor_copy(dst, sm[0:TS, 0:P]).then_inc(s_tok, 1)

            for n in range(NQKV):
                split(n + 1)
                if n:
                    by_rows(n - 1)
                if n in (9, 17):
                    ada_out((n + 5) // 8)
            by_rows(NQKV - 1)

            def feature(n, s):
                kind, _, f = ORDER[n]
                span = slice(s * HALF, (s + 1) * HALF)
                src = ps[s][:, 0:HALF]
                if s == 0:
                    split(n + 1)
                if kind == "u":
                    dve.wait_ge(s_half, 2 * n + s + 1)
                    dve.wait_ge(s_cg, 2 * f + s + 1)
                    dve.tensor_tensor(uT[:, f, 2 + s * HALF:2 + (s + 1) * HALF], src, cgate[:, span],
                                      ALU.mult).then_inc(s_u, 1)
                    if s == 1:
                        dve.wait_ge(s_u, 2 * f + 2)
                        conv(f)
                elif kind == "b":
                    dve.wait_ge(s_half, 2 * n + s + 1)
                    dve.tensor_tensor(yT[:, f, span], src, yT[:, f, span], ALU.mult).then_inc(s_yb, 1)

            def conv(f):
                tap = [ccT[:, f, 2 * TS + j:2 * TS + j + 1] for j in range(3)]
                for dst, src in ((yT[:, f, 0:TP], [uT[:, f, j:j + TP] for j in range(3)]),
                                 (yT[:, f, TP:T], [ccT[:, f, 0:2 * TS:2], ccT[:, f, 1:2 * TS:2],
                                                   uT[:, f, TP + 2:T + 2]])):
                    link(dve.tensor_scalar(dst, src[0], tap[0], None, ALU.mult))
                    for j in (1, 2):
                        link(dve.scalar_tensor_tensor(out=dst, in0=src[j], scalar=tap[j], in1=dst, op0=ALU.mult,
                                                      op1=ALU.add))

            batch_o = {bt[1]: i for i, bt in enumerate(batches) if bt[0] == "o"}
            last_turn = {}
            for i, bt in enumerate(batches):
                if bt[0] == "p":
                    last_turn[bt[1]] = i
            flatS = scS[:, :, 0:323]
            for what, *a in plan:
                if what == "half":
                    feature(*a)
                elif what == "qk":
                    u = a[0]
                    b, h = UNITS[u]
                    off = 0
                    dve.wait_ge(s_bias, 6)
                    if u >= 2:
                        dve.wait_ge(s_pT, last_turn[u - 2] + 1)
                    for g, (lo, n) in enumerate(segments(b)):
                        dve.wait_ge(s_qk, G * no(u) + g + 1)
                        at_b = lo - P * b + P if g == 0 else 256 + 512 * (g - 1) + 384 - P * b + lo
                        dve.tensor_tensor_reduce(prob[:, u % 2, off:off + n], ps[2 + g][:, 0:n],
                                                 bias[:, h, at_b:at_b + n], SCALE, -3.0e38, ALU.add, ALU.max,
                                                 mx[:, 4 * (u % 2) + g:4 * (u % 2) + g + 1]).then_inc(s_sread, 1)
                        off += n
                    dve.wait_ge(s_sread, G * (no(u) + 1))
                    m = mx[:, 4 * (u % 2) + 3:4 * (u % 2) + 4]
                    link(dve.tensor_reduce(m, mx[:, 4 * (u % 2):4 * (u % 2) + 3], AX.X, ALU.max))
                    if u >= 2:
                        dve.wait_ge(s_exp, no(u - 2) + 1)
                    dve.tensor_scalar(negm[:, u % 2:u % 2 + 1], m, -1.0, None, ALU.mult).then_inc(s_neg, 1)
                elif what == "samples":
                    g = a[0]
                    kr = cache[0:KEYS[g], g]
                    dve.wait_ge(s_key, 16 * G)
                    dve.wait_ge(s_qr, 16 * (g + 1))
                    dve.tensor_tensor(kr, kr, qb[0:KEYS[g]], ALU.mult).then_inc(s_kqp, 1)
                    dve.wait_ge(s_kqp, g + 1)
                    dve.tensor_reduce(sc[0:KEYS[g], g], kr.rearrange("p (a d) -> p a d", d=DH), AX.X,
                                      ALU.add).then_inc(s_kq, 1)
                    if g == 0:
                        link(dve.tensor_tensor(qs, qs, ks, ALU.mult))
                        link(dve.tensor_reduce(scS[:, :, 320:323].rearrange("p h g -> p g h"),
                                               qs.rearrange("p (g h d) -> p g h d", g=G, h=H), AX.X, ALU.add))
                elif what == "qs":
                    dve.wait_ge(s_bias, 7)
                    off = 0
                    for g in range(G):
                        dve.wait_ge(s_qk, G * S_AT + g + 1)
                        n = KEYS[g]
                        dve.tensor_tensor(scS[:, :, off:off + n],
                                          ps[2 + g][0:TS, 0:H * n].rearrange("p (h r) -> p h r", h=H),
                                          biasS[:, :, g, 0:n], ALU.add).then_inc(s_sread, 1)
                        off += n
                    dve.wait_ge(s_sread, G * (S_AT + 1))
                    link(dve.tensor_scalar(flatS, flatS, SCALE, None, ALU.mult))
                    link(dve.tensor_reduce(m4[:, 0:4], flatS, AX.X, ALU.max))
                    dve.tensor_tensor(flatS, flatS, m4[:, 0:4].unsqueeze(2).to_broadcast([TS, H, 323]),
                                      ALU.subtract).then_inc(s_neg, 1)
                elif what == "pv" and batches[a[0]][5]:
                    u = batches[a[0]][1]
                    b, h = UNITS[u]
                    dve.wait_ge(s_exp, no(u) + 1)
                    link(dve.reciprocal(rden[:, u % 2:u % 2 + 1], den[:, u % 2:u % 2 + 1]))
                    dve.wait_ge(s_pv, unit_end[u])
                    if h == 0 and b:
                        dve.wait_ge(s_pT, batch_o[b - 1] + 1)
                    dve.tensor_scalar(otok[:, h * DH:(h + 1) * DH], ps[7][:, h * DH:(h + 1) * DH],
                                      rden[:, u % 2:u % 2 + 1], None, ALU.mult).then_inc(s_o, 1)
                if what == "turn_s":
                    dve.wait_ge(s_exp, S_AT + 1)
                    link(dve.tensor_reduce(m4[:, 4:8], flatS, AX.X, ALU.add))
                    link(dve.reciprocal(m4[:, 8:12], m4[:, 4:8]))
                    dve.tensor_tensor(flatS, flatS, m4[:, 8:12].unsqueeze(2).to_broadcast([TS, H, 323]),
                                      ALU.mult).then_inc(s_smp, 1)
                    dve.wait_ge(s_smp, 1)
                    own_p = scS[:, :, 320:323].rearrange("p h g -> p g h").unsqueeze(3).to_broadcast([TS, G, H, DH])
                    own_v = vtok[0:TS, NB]
                    link(dve.tensor_tensor(own_v.rearrange("p (g h d) -> p g h d", g=G, h=H),
                                           own_v.rearrange("p (g h d) -> p g h d", g=G, h=H), own_p, ALU.mult))
                    dve.tensor_reduce(selfs, own_v.rearrange("p (g f) -> p f g", g=G), AX.X, ALU.add
                                      ).then_inc(s_self, 1)
                elif what == "pv_s":
                    dve.wait_ge(s_smpv, 1)
                    dve.tensor_copy(attnT[:, :, TP:T], ps[7][:, 256:256 + 2 * TS].rearrange("p (c b) -> p c b", c=2)
                                    ).then_inc(s_smo, 1)
            for f in range(KD):
                for n in (NCONV + 2 * f, NCONV + 2 * f + 1):
                    if n >= NEARLY:
                        split(n + 1)
                dve.wait_ge(s_sig, 4 * f + 4)
                dve.wait_ge(s_proj, f + 1)
                for s in range(2):
                    span = slice(s * HALF, (s + 1) * HALF)
                    sa, sb_ = sig[:, f % 2, span], sig[:, 2 + f % 2, span]
                    dve.tensor_tensor(sa, ps[2 + s][:, 0:HALF], sa, ALU.mult)
                    ins = dve.tensor_tensor(sb_, ps[4 + s][:, 0:HALF], sb_, ALU.mult)
                link(ins)
                dve.tensor_tensor(mergedT[:, f], sig[:, f % 2], sig[:, 2 + f % 2], ALU.add).then_inc(s_mrg, 1)
            dve.wait_ge(s_modr, 48)
            link(dve.tensor_scalar(mod_p[:, 2], mod_p[:, 2], 1.0, None, ALU.add))
            link(dve.tensor_tensor(mod_p[:, 2], mod_p[:, 2], gffn_b, ALU.mult))
            link(dve.tensor_scalar(mod_s[:, 2], mod_s[:, 2], 1.0, None, ALU.add))
            link(dve.tensor_tensor(mod_s[:, 2], mod_s[:, 2], gffn_b[0:TS], ALU.mult))
            dve.engine_nop().then_inc(s_gfu, 1)
            for n, i in enumerate(RB):
                r = rows[i]
                md = mod_p if i < 4 else mod_s
                h2 = h2t[0:r, n % 2]
                if n >= 2:
                    dve.wait_ge(s_h2w[n % 2], 16 * (n // 2))
                    dve.wait_ge(s_h2T, 2 * (n - 1))
                if n == 0:
                    dve.wait_ge(s_mrg, KD)
                for c in range(2):
                    half = slice(512 * c, 512 * (c + 1))
                    dve.wait_ge(s_wom, 2 * n + c + 1)
                    src = ps[2 + 2 * (n % 2) + c][0:r]
                    if n == 0 and c == 1:
                        src = h2[:, half]
                        link(dve.tensor_copy(src, ps[3][R:R + r]))
                    link(dve.tensor_tensor(h2[:, half], src, md[0:r, 0, half], ALU.mult))
                dve.wait_ge(s_xr[i], 16)
                dve.tensor_tensor(x[0:r, i], x[0:r, i], h2, ALU.add).then_inc(s_x2, 1)
                dve.wait_ge(s_sq2, n + 1)
                dve.tensor_scalar(rstd[0:r, i:i + 1], ssq[0:r, i:i + 1], 1.0 / D, EPS, ALU.mult, ALU.add).then_inc(s_ms, 1)
                dve.wait_ge(s_rstd, 5 + n + 1)
                link(dve.scalar_tensor_tensor(out=h2, in0=x[0:r, i], scalar=rstd[0:r, i:i + 1], in1=md[0:r, 2],
                                              op0=ALU.mult, op1=ALU.mult))
                dve.tensor_tensor(h2, h2, md[0:r, 1], ALU.add).then_inc(s_h2, 1)

            def wide(ap, n):
                return ap.unsqueeze(len(ap.shape)).to_broadcast([*ap.shape, n])

            dve.wait_ge(s_h2, 5)
            dve.memset(past[:, 0], 0.0)
            link(dve.memset(lgt.rearrange("p t e -> p (t e)"), 0.0))
            dve.wait_ge(s_rt, 5)
            dve.wait_ge(s_rc, 32)
            for n, i in enumerate(RB):
                r = rows[i]
                ins = dve.tensor_tensor(lgt[0:r, i], ps[0][0:r, 64 * n:64 * n + 36], rbias[0:r], ALU.add)
            link(ins)
            lg, le = lgt[:, :, 0:NG], lgt[:, :, NG:NG + NE].rearrange("p t (g e) -> p t g e", g=NG)

            def first_of(dst, vals, top, n):
                eq = geq[:, :, 0:n]
                link(dve.tensor_tensor(eq, vals, wide(top, n), ALU.is_equal))
                link(dve.tensor_scalar(eq, eq, -64.0, None, ALU.mult))
                link(dve.tensor_tensor(eq, eq, iota_e[:, 0:n].unsqueeze(1).to_broadcast([P, 5, n]), ALU.add))
                link(dve.tensor_reduce(dst, eq, AX.X, ALU.min))
                link(dve.tensor_scalar(dst, dst, 64.0, None, ALU.add))

            link(dve.tensor_reduce(gmax, lg, AX.X, ALU.max))
            dve.tensor_tensor(gexp, lg, wide(gmax, NG), ALU.subtract).then_inc(s_rw, 1)
            first_of(gidx, lg, gmax, NG)
            link(dve.tensor_tensor(goh, iota_e[:, 0:NG].unsqueeze(1).to_broadcast([P, 5, NG]), wide(gidx, NG),
                                   ALU.is_equal))
            for i in range(5):
                ins = dve.tensor_tensor(prod[:, i], le[:, i], wide(goh[:, i], EG), ALU.mult)
            link(ins)
            link(dve.tensor_reduce(sel, prod.rearrange("p t g e -> p t e g"), AX.X, ALU.add))
            link(dve.tensor_reduce(vk[:, 0], sel, AX.X, ALU.max))
            first_of(ik[:, 0], sel, vk[:, 0], EG)
            link(dve.tensor_tensor(geq, iota_e[:, 0:EG].unsqueeze(1).to_broadcast([P, 5, EG]), wide(ik[:, 0], EG),
                                   ALU.is_equal))
            link(dve.scalar_tensor_tensor(out=sel, in0=geq, scalar=-BIG, in1=sel, op0=ALU.mult, op1=ALU.add))
            link(dve.tensor_reduce(vk[:, 1], sel, AX.X, ALU.max))
            first_of(ik[:, 1], sel, vk[:, 1], EG)
            dve.tensor_tensor(wk[:, 1], vk[:, 1], vk[:, 0], ALU.subtract).then_inc(s_rw, 1)
            for k in range(2):
                link(dve.scalar_tensor_tensor(out=ek[:, k], in0=gidx, scalar=float(EG), in1=ik[:, k], op0=ALU.mult,
                                              op1=ALU.add))
            link(dve.tensor_tensor(ohe, iota_e[:, 0:NE].unsqueeze(1).unsqueeze(1).to_broadcast([P, 2, 5, NE]),
                                   wide(ek, NE), ALU.is_equal))
            link(dve.tensor_tensor(member, ohe[:, 0], ohe[:, 1], ALU.add))
            link(dve.tensor_tensor(member, member, wide(valid, NE), ALU.mult))
            link(dve.tensor_copy(past[:, 1], member[:, 0]))
            for i in range(1, 5):
                link(dve.tensor_tensor(past[:, i + 1], past[:, i], member[:, i], ALU.add))
            dve.engine_nop().then_inc(s_rw, 1)
            for k in range(2):
                link(dve.tensor_scalar(code[:, k], tok1, 2.0, float(k - 1), ALU.mult, ALU.add))
                link(dve.tensor_tensor(code[:, k], code[:, k], valid, ALU.mult))
            dve.wait_ge(s_rp, 1)
            dve.tensor_copy(ranks, cube(ps[2][:, 0:5 * NE], 5))
            link(dve.tensor_copy(count, ps[2][:, 5 * NE:6 * NE]))
            link(dve.tensor_scalar(extra_i, count, float(R - 1), None, ALU.add))
            link(dve.tensor_scalar(extra_i, extra_i, RBITS, None, ALU.arith_shift_right))
            link(dve.tensor_scalar(extra, extra_i, -1.0, None, ALU.add))
            link(dve.tensor_scalar(extra, extra, 0.0, None, ALU.max))
            link(dve.tensor_tensor_scan(upto, extra, extra, 0.0, ALU.add, ALU.bypass))
            link(dve.tensor_tensor(before, upto, extra, ALU.subtract))
            link(dve.tensor_tensor(tmp2, ohe, ranks.unsqueeze(1).to_broadcast([P, 2, 5, NE]), ALU.mult))
            link(dve.tensor_reduce(rk, tmp2, AX.X, ALU.add))
            link(dve.tensor_tensor(tmp2, ohe, before.unsqueeze(1).unsqueeze(1).to_broadcast([P, 2, 5, NE]), ALU.mult))
            link(dve.tensor_reduce(bk, tmp2, AX.X, ALU.add))
            link(dve.tensor_copy(rank_i, rk))
            link(dve.tensor_scalar(rank_i, rank_i, R - 1, None, ALU.bitwise_and))
            link(dve.tensor_copy(slotk, rank_i))
            link(dve.tensor_tensor(qk_, rk, slotk, ALU.subtract))
            link(dve.tensor_scalar(qk_, qk_, 1.0 / R, None, ALU.mult))
            link(dve.tensor_tensor(tilek, bk, qk_, ALU.add))
            link(dve.tensor_scalar(tilek, tilek, float(NE - 1), None, ALU.add))
            link(dve.tensor_tensor(tilek, tilek, ek, ALU.subtract))
            link(dve.tensor_scalar(t10, qk_, 0.5, None, ALU.is_gt))
            link(dve.tensor_tensor(tilek, tilek, t10, ALU.mult))
            link(dve.tensor_tensor(tilek, tilek, ek, ALU.add))
            dve.tensor_tensor(oh_slot, slot_i.unsqueeze(1).unsqueeze(1).to_broadcast([P, 2, 5, P]), wide(slotk, P),
                              ALU.is_equal)
            link(dve.tensor_tensor(oh_tile, iota_e.unsqueeze(1).unsqueeze(1).to_broadcast([P, 2, 5, NTILE]),
                                   wide(tilek, NTILE), ALU.is_equal))
            dve.tensor_tensor(oh_val[:, :, :, 0:NTILE], oh_tile, wide(code, NTILE), ALU.mult)
            for k in range(2):
                ins = dve.tensor_tensor(oh_val[:, k, :, NTILE:2 * NTILE], oh_tile[:, k], wide(tok1, NTILE), ALU.mult)
            ins.then_inc(s_rw, 1)
            dve.wait_ge(s_ra, 2)
            link(dve.tensor_reduce(ptop, gexp, AX.X, ALU.add))
            link(dve.scalar_tensor_tensor(out=wk[:, 0], in0=wk[:, 1], scalar=1.0, in1=ptop, op0=ALU.add,
                                          op1=ALU.mult))
            link(dve.reciprocal(wk[:, 0], wk[:, 0]))
            link(dve.tensor_tensor(wk[:, 1], wk[:, 1], wk[:, 0], ALU.mult))
            link(dve.tensor_tensor(owner_c[0:1], upto[0:1].unsqueeze(1).to_broadcast([1, OVER, NE]),
                                   iota_e[0:1, 0:OVER].unsqueeze(2).to_broadcast([1, OVER, NE]), ALU.is_le))
            link(dve.tensor_reduce(owner_f[0:1], owner_c[0:1], AX.X, ALU.add))
            link(dve.tensor_scalar(owner_f[0:1], owner_f[0:1], float(NE - 1), None, ALU.min))
            dve.tensor_copy(owner[0:1], owner_f[0:1])
            link(dve.tensor_copy(nover[0:1], upto[0:1, NE - 1:NE]))
            dve.wait_ge(s_rp, 2)
            link(dve.tensor_copy(lists_f, ps[3][:, 0:2 * NTILE]))
            link(dve.tensor_scalar(empty, lists_f, 0.0, SKIP, ALU.is_equal, ALU.mult))
            link(dve.scalar_tensor_tensor(out=lists_f, in0=lists_f, scalar=2.0, in1=empty, op0=ALU.mult, op1=ALU.add))
            link(dve.tensor_scalar(lists_f, lists_f, -2.0, jcol, ALU.add, ALU.add))
            dve.tensor_copy(lists.rearrange("p a b -> p (a b)"), lists_f).then_inc(s_lists, 1)

            def act_of(e, j):
                b = j % 2
                dve.wait_ge(s_si, e + 1)
                at_least(dve, s_ta, e - 1)
                dve.tensor_tensor(actv[:, b], ps[2 + b][:, P:2 * P], silu[:, b], ALU.mult).then_inc(s_am, 1)

            def act_turned(e, j):
                b = j % 2
                dve.wait_ge(s_ta, e + 1)
                at_least(dve, s_y, e - 1)
                dve.tensor_copy(actT[:, b], ps[4][:, 0:P]).then_inc(s_at, 1)

            def down_of(e, j, written):
                b = j % 2
                dve.wait_ge(s_y, e + 1)
                at_least(dve, s_sc[b], written)
                dve.tensor_copy(ys[:, b], ps[5 + b][:]).then_inc(s_ye, 1)

            def four(it):
                e0 = EUN * it
                for j in range(EUN):
                    act_of(e0 + j, j)
                    if j or not isinstance(it, int) or it:
                        down_of(e0 + (j - 1), j - 1, 8 * e0 + 16 * ((j - 1) // 2))
                    act_turned(e0 + j, j)

            four(0)
            with dve.Fori(1, NE // EUN) as it:
                four(it)
            down_of(NE - 1, NE - 1, 8 * NE - 16)
            n_over = dve.value_load(nover[0:1, 0:1], min_val=0, max_val=OVER)
            with dve.If(n_over > 0):
                with dve.Fori(0, n_over) as o:
                    act_of(o + NE, 0)
                    act_turned(o + NE, 0)
                    down_of(o + NE, 0, 16 * o + 16 * (NE // 2))
            def mixed(n):
                i = RB[n]
                r = rows[i]
                pair = yk[:, i] if i < 4 else yk_s
                dve.wait_ge(s_w0, n + 1)
                if n >= 2:
                    dve.wait_ge(s_sq3, n - 1)
                dve.scalar_tensor_tensor(out=mix[0:r, n % 2], in0=pair[0:r, 1], scalar=wk[0:r, 1, i:i + 1],
                                         in1=pair[0:r, 0], op0=ALU.mult, op1=ALU.add).then_inc(s_mix, 1)

            def summed(n):
                i = RB[n]
                r = rows[i]
                dve.wait_ge(s_mixg, n + 1)
                dve.tensor_tensor(x[0:r, i], x[0:r, i], mix[0:r, n % 2], ALU.add).then_inc(s_x3, 1)

            def mean_square(n):
                i = RB[n]
                r = rows[i]
                dve.wait_ge(s_sq3, n + 1)
                dve.tensor_scalar(rstd[0:r, i:i + 1], ssq[0:r, i:i + 1], 1.0 / D, EPS, ALU.mult, ALU.add
                                  ).then_inc(s_ms, 1)

            def normed(n):
                i = RB[n]
                r = rows[i]
                dve.wait_ge(s_rstd, 10 + n + 1)
                dve.wait_ge(s_gf, 16)
                if n >= 2:
                    dve.wait_ge(s_out[n % 2], 16 * (n // 2))
                dve.scalar_tensor_tensor(out=res[0:r, n % 2], in0=x[0:r, i], scalar=rstd[0:r, i:i + 1],
                                         in1=gfin_b[0:r], op0=ALU.mult, op1=ALU.mult).then_inc(s_res, 1)

            mixed(0)
            for n in range(5):
                if n + 1 < 5:
                    mixed(n + 1)
                if n:
                    mean_square(n - 1)
                summed(n)
                if n:
                    normed(n - 1)
            mean_square(4)
            normed(4)

        @block.tensor
        def _(pe):
            pe.wait_ge(s_ident, 1)
            pe.wait_ge(s_csilu, 1)
            idn = ident
            for k in range(KD):
                pe.transpose(ps[2][:, 32 * k:32 * k + 1 + TS], crow[:, k * P:(k + 1) * P], idn[0:1 + TS, 0:1 + TS])
            for f in range(CF):
                pe.transpose(ps[3][:, 32 * f:32 * f + 19], ccrow[:, f * P:(f + 1) * P], idn[0:19, 0:19])
            pe.transpose(ps[3][:, 32 * CF:32 * CF + KD], g8, idn[0:KD, 0:KD]).then_inc(s_cT, 1)
            pe.wait_ge(s_cvec, 1)

            def ada_step(a):
                w = ada0[a] if a < 4 else ada
                pe.wait_ge(s_ada[min(a, 3)], 32 * (1 + max(0, a - 3)))
                g, first = a // 4, 2 * (a % 4)
                if first == 0:
                    at_least(pe, s_adaev, g - 1)
                for k in (first, first + 1):
                    for j in range(4):
                        ins = pe.matmul(ps[6 + g % 2][32 * j:32 * j + 32, :], cvec[:, k],
                                        w[:, k - first, 512 * j:512 * j + 512],
                                        start=(k == 0), stop=(k == KD - 1), skip_group_check=True)
                ins.then_inc(s_adamm, 1)

            def turn_x(k):
                at_least(pe, s_hA, k - 4)
                for i in range(NB):
                    ins = pe.transpose(ps[TURNED[k % 5]][:, i * P:(i + 1) * P], x[:, i, k * P:(k + 1) * P], idn)
                ins.then_inc(s_xT, 1)

            for a in range(3):
                ada_step(a)
            pe.wait_ge(s_xn, 5)
            for k in range(KD):
                ins = pe.transpose(ps[3][:, k * TS:(k + 1) * TS], x[0:TS, 4, k * P:(k + 1) * P], idn[0:TS, 0:TS])
            ins.then_inc(s_xT, 1)
            for k in range(3):
                turn_x(k)
            ada_step(3)
            turn_x(3)
            turn_x(4)
            pe.wait_ge(s_adaev, 1)
            for cc in range(4):
                ins = pe.transpose(ps[0][:, cc * P:(cc + 1) * P], mods[:, cc], idn)
            ins.then_inc(s_modT, 1)
            for k in range(5, KD):
                turn_x(k)
            pe.wait_ge(s_hA, KD)
            pe.wait_ge(s_hD, KD + 1)

            def tile_read(n, s):
                kind, _, f = ORDER[n]
                if kind in "vkq":
                    pe.wait_ge(s_feat, 2 * n + s + 1)
                elif kind == "c":
                    pe.wait_ge(s_cg, 2 * f + s + 1)
                elif kind == "u":
                    pe.wait_ge(s_u, 2 * f + s + 1)
                elif kind == "b":
                    pe.wait_ge(s_yb, 2 * f + s + 1)
                else:
                    pe.wait_ge(s_sig, 2 * (n - NCONV) + s + 1)

            def half(n, s):
                pe.wait_ge(s_whi, n + 1)
                pe.wait_ge(s_wlo, n + 1)
                if n:
                    tile_read(n - 1, s)
                for k in range(KD):
                    for wp, hp in ((0, 1), (0, 0), (1, 0)):
                        ins = pe.matmul(ps[s][:, 0:HALF], w_parts[:, n % 2, wp, k],
                                        h_parts[:, hp, k, s * HALF:(s + 1) * HALF],
                                        start=(k == 0 and hp == 1), stop=(k == KD - 1 and wp == 1))
                ins.then_inc(s_half, 1)

            def to_rows(n):
                kind, _, f = ORDER[n]
                pe.wait_ge(s_feat, 2 * n + 2)
                at_least(pe, s_tok, n - 1)
                src = {"v": vst[:, n % 2], "k": kT[:, f], "q": qT[:, f]}[kind]
                if kind != "q":
                    for b in range(NB):
                        pe.transpose(ps[2 + 2 * (n % 2)][:, b * P:(b + 1) * P], src[:, b * P:(b + 1) * P], idn)
                pe.transpose(ps[3 + 2 * (n % 2)][0:TS, 0:P], src[:, TP:T], idn).then_inc(s_tokT, 1)

            for n in range(NQKV):
                for s in range(2):
                    half(n, s)
                if n:
                    to_rows(n - 1)
                if n % 2 == 1 and 4 <= (n + 5) // 2 < 12:
                    ada_step((n + 5) // 2)
            to_rows(NQKV - 1)
            pe.wait_ge(s_tok, NQKV)

            for what, *a in plan:
                if what == "half":
                    half(*a)
                elif what == "qk":
                    u = a[0]
                    b, h = UNITS[u]
                    for g, (lo, n) in enumerate(segments(b)):
                        at_least(pe, s_sread, G * (no(u) - 1) + g + 1)
                        f, p0 = 2 * g + h // 2, DH * (h % 2)
                        pe.matmul(ps[2 + g][:, 0:n], qT[p0:p0 + DH, f, b * P:(b + 1) * P], kT[p0:p0 + DH, f, lo:lo + n],
                                  start=True, stop=True).then_inc(s_qk, 1)
                elif what == "qs":
                    pe.wait_ge(s_kq, G)
                    for g in range(G):
                        n = KEYS[g]
                        pe.wait_ge(s_sread, G * (S_AT - 1) + g + 1)
                        for h in range(H):
                            ins = pe.transpose(ps[2 + g][0:TS, h * n:(h + 1) * n], sc[0:n, g, h::H], idn[0:n, 0:n])
                        ins.then_inc(s_qk, 1)
                elif what.startswith("turn"):
                    i = a[0]
                    at_least(pe, s_odd if i % 2 else s_even, i // 2)
                    bank = ps[5 + i % 2]
                    bt = batches[i]
                    if what == "turn":
                        _, u, first, chunks, _, _ = bt
                        pe.wait_ge(s_exp, no(u) + 1)
                        for c in range(len(chunks)):
                            ins = pe.transpose(bank[:, c * P:(c + 1) * P],
                                               prob[:, u % 2, (first + c) * P:(first + c + 1) * P], idn)
                    elif what == "turn_o":
                        pe.wait_ge(s_o, H * (bt[1] + 1))
                        for c in range(2):
                            ins = pe.transpose(bank[:, c * P:(c + 1) * P], otok[:, c * P:(c + 1) * P], idn)
                    elif what == "turn_s":
                        pe.wait_ge(s_smp, 1)
                        off = 0
                        for g in range(G):
                            n = KEYS[g]
                            for h in range(H):
                                ins = pe.transpose(bank[0:n, (g * H + h) * TS:(g * H + h + 1) * TS],
                                                   scS[:, h, off:off + n], idn[0:TS, 0:TS])
                            off += n
                    else:
                        pe.wait_ge(s_u, 2 * CF)
                        for f in range(CF):
                            ins = pe.transpose(bank[0:2 + TS, f * P:(f + 1) * P], uT[:, f, TP:T + 2], idn)
                    ins.then_inc(s_pT, 1)
                elif what == "pv":
                    i = a[0]
                    _, u, first, chunks, is_first, is_last = batches[i]
                    b, h = UNITS[u]
                    pe.wait_ge(s_odd if i % 2 else s_even, i // 2 + 1)
                    if is_first:
                        at_least(pe, s_o, u)
                        if u == S_AT + 1:
                            pe.wait_ge(s_smo, 1)
                    for c, (g, kb) in enumerate(chunks):
                        ins = pe.matmul(ps[7][:, h * DH:(h + 1) * DH], probT[:, i % 2, c * P:(c + 1) * P],
                                        vtok[:, kb, g * OW + h * DH:g * OW + (h + 1) * DH],
                                        start=(is_first and c == 0), stop=(is_last and c == len(chunks) - 1),
                                        skip_group_check=True)
                    ins.then_inc(s_pv, 1)
                elif what == "pv_s":
                    i = [m for m, bt in enumerate(batches) if bt[0] == "s"][0]
                    pe.wait_ge(s_odd if i % 2 else s_even, i // 2 + 1)
                    pe.wait_ge(s_self, 1)
                    pe.wait_ge(s_val, 16 * G)
                    pe.wait_ge(s_o, S_AT + 1)
                    for c in range(2):
                        pe.matmul(ps[7][:, 256 + c * TS:256 + (c + 1) * TS], selfs[:, c * P:(c + 1) * P],
                                  idn[0:TS, 0:TS], start=(c == 0), stop=False, skip_group_check=True)
                    for g in range(G):
                        n = KEYS[g]
                        val = cache[0:n, g].rearrange("p (b h d) -> p b h d", b=TS, h=H)
                        for h in range(H):
                            c, p0 = h // 2, DH * (h % 2)
                            for b in range(TS):
                                ins = pe.matmul(ps[7][p0:p0 + DH, 256 + c * TS + b:256 + c * TS + b + 1],
                                                val[:, b, h], smT[0:n, g * H + h, b:b + 1], start=False,
                                                stop=(g == G - 1), skip_group_check=True)
                    ins.then_inc(s_smpv, 1)

            pe.wait_ge(s_wp, 32)
            pe.wait_ge(s_smo, 1)
            n_b = len(batches)
            pe.wait_ge(s_even, (n_b + 1) // 2)
            pe.wait_ge(s_odd, n_b // 2)
            for f in range(KD):
                for n in (NCONV + 2 * f, NCONV + 2 * f + 1):
                    if n >= NEARLY:
                        for s in range(2):
                            half(n, s)
                if f:
                    pe.wait_ge(s_mrg, f)
                for s in range(2):
                    span = slice(s * HALF, (s + 1) * HALF)
                    for c in range(2):
                        pe.matmul(ps[2 + s][:, 0:HALF], wpa[:, c, f * P:(f + 1) * P], attnT[:, c, span],
                                  start=(c == 0), stop=(c == 1))
                    for c in range(CF):
                        ins = pe.matmul(ps[4 + s][:, 0:HALF], wpb[:, c, f * P:(f + 1) * P], yT[:, c, span],
                                        start=(c == 0), stop=(c == CF - 1))
                ins.then_inc(s_proj, 1)
            pe.wait_ge(s_mrg, KD)
            pe.wait_ge(s_wo, 32)

            def router(n):
                r = rows[RB[n]]
                pe.wait_ge(s_h2, n + 1)
                for c in range(2):
                    at_least(pe, s_h2c, 2 * (n - 1) + c + 1)
                    for k in range(4):
                        ins = pe.transpose(ps[6 + c][:, k * P:k * P + r],
                                           h2t[0:r, n % 2, (4 * c + k) * P:(4 * c + k + 1) * P], idn[0:r, 0:r])
                    ins.then_inc(s_h2T, 1)
                pe.wait_ge(s_h2c, 2 * n + 2)
                for k in range(KD):
                    ins = pe.matmul(ps[0][0:r, 64 * n:64 * n + 36], h2T[:, k, 0:r], wrt[:, k], start=(k == 0),
                                    stop=(k == KD - 1), skip_group_check=True)
                ins.then_inc(s_rt, 1)

            pe.wait_ge(s_wr, 32)
            for n, i in enumerate(RB):
                r = rows[i]
                at_least(pe, s_x2, n - 1)
                if n == 0:
                    for k in range(KD):
                        for c in range(2):
                            ins = pe.matmul(ps[2 + c][R * c:R * c + r], mergedT[:, k, TP:T], wo[c][:, k],
                                            start=(k == 0), stop=(k == KD - 1), skip_group_check=True)
                            if k == KD - 1:
                                ins.then_inc(s_wom, 1)
                    continue
                for c in range(2):
                    for k in range(KD):
                        ins = pe.matmul(ps[2 + 2 * (n % 2) + c][0:r], mergedT[:, k, i * P:i * P + r], wo[c][:, k],
                                        start=(k == 0), stop=(k == KD - 1))
                    ins.then_inc(s_wom, 1)
                    if n and c == 0:
                        router(n - 1)
            router(4)
            pe.wait_ge(s_rw, 3)
            pe.matmul(ps[2][:, 0:6 * NE], ones, past.rearrange("p t e -> p (t e)"), start=True, stop=False,
                      skip_group_check=True)
            pe.matmul(ps[2][:, 0:5 * NE], upper, member.rearrange("p t e -> p (t e)"), start=False, stop=True,
                      skip_group_check=True).then_inc(s_rp, 1)
            pe.wait_ge(s_rw, 4)
            for k in range(2):
                for i in range(5):
                    ins = pe.matmul(ps[3][:, 0:2 * NTILE], oh_slot[:, k, i], oh_val[:, k, i], start=(k == 0 and i == 0),
                                    stop=(k == 1 and i == 4))
            ins.then_inc(s_rp, 1)
            pe.wait_ge(s_lists, 1)

            def turn_rows(e, j, gathered):
                b = j % 2
                pe.wait_ge(s_hg[j % EUN], gathered)
                at_least(pe, s_te, e - 1)
                for c in range(4):
                    ins = pe.transpose(ps[b][:, c * P:(c + 1) * P], hg[:, j % EUN, c::4], idn)
                ins.then_inc(s_t, 1)

            def gate_up(e, j, slot, loaded):
                b = j % 2
                pe.wait_ge(s_te, e + 1)
                pe.wait_ge(s_eg[slot], loaded)
                at_least(pe, s_am, e - 1)
                for jj in range(2):
                    for c in range(4):
                        for hh in range(2):
                            ins = pe.matmul(ps[2 + b][R * hh:R * hh + R, 0:2 * P],
                                            hTe[:, b, c * P + jj * R:c * P + jj * R + R],
                                            w_gu[slot][:, 4 * jj + c, :, hh * P:(hh + 1) * P],
                                            start=(jj == 0 and c == 0), stop=(jj == 1 and c == 3),
                                            skip_group_check=True)
                ins.then_inc(s_gu, 1)

            def turn_act(e, j):
                pe.wait_ge(s_am, e + 1)
                at_least(pe, s_at, e)
                pe.transpose(ps[4][:, 0:P], actv[:, j % 2], idn).then_inc(s_ta, 1)

            def down(e, j, slot, loaded):
                b = j % 2
                pe.wait_ge(s_at, e + 1)
                pe.wait_ge(s_ed[slot], loaded)
                at_least(pe, s_ye, e - 1)
                for hh in range(2):
                    for jj in range(2):
                        ins = pe.matmul(ps[5 + b][R * jj:R * jj + R], actT[:, b, hh * R:hh * R + R],
                                        w_dn[slot][:, hh, 512 * jj:512 * jj + 512], start=(hh == 0), stop=(hh == 1),
                                        skip_group_check=True)
                ins.then_inc(s_y, 1)

            def four(it, last=False):
                e0 = EUN * it
                for j in range(EUN):
                    if not last or j + 1 < EUN:
                        turn_rows(e0 + (j + 1), j + 1, 16 * it + 16 * ((j + 1) // EUN + 1))
                    gate_up(e0 + j, j, j, 64 * it + 64)
                    if j or not isinstance(it, int) or it:
                        down(e0 + (j - 1), j - 1, (j - 1) % EUN, 16 * it + (16 if j else 0))
                    turn_act(e0 + j, j)

            turn_rows(0, 0, 16)
            four(0)
            with pe.Fori(1, NE // EUN - 1) as it:
                four(it)
            four(NE // EUN - 1, True)
            down(NE - 1, NE - 1, EUN - 1, 16 * (NE // EUN))
            n_over = pe.value_load(nover[0:1, 0:1], min_val=0, max_val=OVER)
            with pe.If(n_over > 0):
                with pe.Fori(0, n_over) as o:
                    turn_rows(o + NE, 0, 16 * o + (16 * (NE // EUN) + 16))
                    gate_up(o + NE, 0, 0, 64 * o + (64 * (NE // EUN) + 64))
                    turn_act(o + NE, 0)
                    down(o + NE, 0, 0, 16 * o + (16 * (NE // EUN) + 16))


_INS = ["x_prompt", "x_sample", "cache_kv_w128", "cache_kv_w512", "cache_kv_w2048", "cache_conv", "c_prompt",
        "c_sample", "g_mix", "w_ada", "b_ada", "w_in", "conv_w", "w_pa", "w_pb", "w_o", "g_ffn", "w_router_group",
        "b_router_group", "w_router_expert", "b_router_expert", "w_gate_e", "w_up_e", "w_down_e", "g_final"]
_OUTS = [(1, TP, D), (TS, 1, D), (1, 1, 128, 2, H, DH), (1, 1, 512, 2, H, DH), (1, 1, 512, 2, H, DH),
         (1, 1, 2, CW), (1, TS, 1, 2, H, DH), (1, TS, 1, 2, H, DH), (1, TS, 1, 2, H, DH), (1, TS, 2, CW)]


def kernel(**inputs):
    import concourse.bacc as bacc
    from concourse.bass_utils import run_bass_kernel_spmd

    nc = bacc.Bacc("TRN2", target_bir_lowering=False, num_devices=1)
    arrays, args = {}, []
    for name in _INS:
        a = np.ascontiguousarray(inputs[name])
        arrays[f"in_{name}"] = a
        args.append(nc.dram_tensor(f"in_{name}", a.shape, mybir.dt.from_np(a.dtype), kind="ExternalInput").ap())
    for i, shape in enumerate(_OUTS):
        args.append(nc.dram_tensor(f"out_{i}", shape, F32, kind="ExternalOutput").ap())
    hybrid_step(nc, *args)
    r = run_bass_kernel_spmd(nc, [arrays], core_ids=[0])
    return tuple(r.results[0][f"out_{i}"] for i in range(len(_OUTS)))
```
